# Optimizing a Trainium2 kernel written in Bass

```python
import math
import jax, jax.numpy as jnp
from jax import lax
import numpy as np

D_MODEL = 2048
BATCH = 1
SEQ = 256
DEPTH = 1

ATTN_HEADS = 8
ATTN_QK_DIM = 64
ATTN_V_DIM = 2 * ATTN_QK_DIM
ATTN_WIDTH = ATTN_HEADS * ATTN_V_DIM
Q_BLOCK = 128
SSM_WIDTH = D_MODEL // 2
SSM_GROUP = 16
SSM_GROUPS = SSM_WIDTH // SSM_GROUP
SSM_STATE = 64
DT_MIN = 1e-3
DT_MAX = 1e-1
N_EXPERT_GROUPS = 4
EXPERTS_PER_GROUP = 4
N_EXPERTS = N_EXPERT_GROUPS * EXPERTS_PER_GROUP
TOP_K_INNER = 2
EXPERT_FF = D_MODEL // 2
RMS_EPS = 1e-6

Q_OFF = 0
K_OFF = Q_OFF + ATTN_WIDTH
V_OFF = K_OFF + ATTN_WIDTH
U_OFF = V_OFF + ATTN_WIDTH
GA_OFF = U_OFF + SSM_WIDTH
GB_OFF = GA_OFF + D_MODEL
IN_COLS = GB_OFF + D_MODEL

kernel_name = "hybrid_diffattn_s5_hmoe_encoder"

def rmsnorm(x, g):
    xf = x.astype(jnp.float32)
    y = xf * lax.rsqrt(jnp.mean(xf * xf, axis=-1, keepdims=True) + RMS_EPS)
    return (y * g.astype(jnp.float32)).astype(x.dtype)

def diff_attention(q, k, v, q_gain, k_gain, lam, slopes):
    B, S, H = q.shape[0], q.shape[1], q.shape[2]
    scale = ATTN_QK_DIM ** -0.5
    qf = rmsnorm(q, q_gain).astype(jnp.float32) * scale
    kf = rmsnorm(k, k_gain).astype(jnp.float32)
    vf = v.astype(jnp.float32)
    nb = S // Q_BLOCK
    qb = qf.reshape(B, nb, Q_BLOCK, H, 2, ATTN_QK_DIM).transpose(1, 0, 2, 3, 4, 5)
    kpos = jnp.arange(S, dtype=jnp.float32)

    def block(args):
        qi, i = args
        qpos = (i * Q_BLOCK + jnp.arange(Q_BLOCK)).astype(jnp.float32)
        dist = jnp.abs(qpos[:, None] - kpos[None, :])
        bias = -slopes[:, None, None, None] * dist[None, None]
        s = jnp.einsum('bqhcd,bkhcd->bhcqk', qi, kf) + bias
        p = jax.nn.softmax(s, axis=-1)
        w = p[:, :, 0] - lam * p[:, :, 1]
        return jnp.einsum('bhqk,bkhe->bqhe', w, vf)

    out = lax.map(block, (qb, jnp.arange(nb)))
    return out.transpose(1, 0, 2, 3, 4).reshape(B, S, H, ATTN_V_DIM)

def s5_direction(ug, lam_re, lam_im, log_dt, b_re, b_im, c_re, c_im, reverse):
    S = ug.shape[1]
    dt = jnp.exp(log_dt.astype(jnp.float32))[:, None]
    lr = lam_re.astype(jnp.float32)
    li = lam_im.astype(jnp.float32)
    mag = jnp.exp(lr * dt)
    a_re = mag * jnp.cos(li * dt)
    a_im = mag * jnp.sin(li * dt)
    nr = a_re - 1.0
    den = lr * lr + li * li
    f_re = (nr * lr + a_im * li) / den
    f_im = (a_im * lr - nr * li) / den
    br = b_re.astype(jnp.float32)
    bi = b_im.astype(jnp.float32)
    bb_re = f_re[..., None] * br - f_im[..., None] * bi
    bb_im = f_re[..., None] * bi + f_im[..., None] * br
    bu_re = jnp.einsum('gnp,bsgp->bsgn', bb_re, ug)
    bu_im = jnp.einsum('gnp,bsgp->bsgn', bb_im, ug)
    a_re_s = jnp.broadcast_to(a_re[None, None], (1, S) + a_re.shape)
    a_im_s = jnp.broadcast_to(a_im[None, None], (1, S) + a_im.shape)

    def combine(e1, e2):
        a1r, a1i, b1r, b1i = e1
        a2r, a2i, b2r, b2i = e2
        return (a1r * a2r - a1i * a2i,
                a1r * a2i + a1i * a2r,
                a2r * b1r - a2i * b1i + b2r,
                a2r * b1i + a2i * b1r + b2i)

    _, _, h_re, h_im = lax.associative_scan(
        combine, (a_re_s, a_im_s, bu_re, bu_im), reverse=reverse, axis=1)
    return (jnp.einsum('gpn,bsgn->bsgp', c_re.astype(jnp.float32), h_re)
            - jnp.einsum('gpn,bsgn->bsgp', c_im.astype(jnp.float32), h_im))

def s5_bidirectional(u, lam_re, lam_im, log_dt, b_re, b_im, c_re, c_im, d_skip, w_glu):
    B, S, W = u.shape
    ug = u.astype(jnp.float32).reshape(B, S, SSM_GROUPS, SSM_GROUP)
    y_f = s5_direction(ug, lam_re[0], lam_im[0], log_dt[0], b_re[0], b_im[0],
                       c_re[0], c_im[0], False)
    y_b = s5_direction(ug, lam_re[1], lam_im[1], log_dt[1], b_re[1], b_im[1],
                       c_re[1], c_im[1], True)
    d = d_skip.astype(jnp.float32).reshape(SSM_GROUPS, SSM_GROUP)
    y = (y_f + y_b + d * ug).reshape(B, S, W)
    y = jax.nn.gelu(y).astype(u.dtype)
    return y * jax.nn.sigmoid(y @ w_glu)

def hybrid_mixer(xn, layer_idx, slopes, w_in, q_gain, k_gain, lam_q1, lam_k1, lam_q2,
                 lam_k2, head_gain, w_attn_up, ssm_lam_re, ssm_lam_im, ssm_log_dt,
                 ssm_b_re, ssm_b_im, ssm_c_re, ssm_c_im, ssm_d, w_glu, w_ssm_up, w_out):
    B, S, _ = xn.shape
    h = xn @ w_in
    q = h[..., Q_OFF:K_OFF].reshape(B, S, ATTN_HEADS, 2, ATTN_QK_DIM)
    k = h[..., K_OFF:V_OFF].reshape(B, S, ATTN_HEADS, 2, ATTN_QK_DIM)
    v = h[..., V_OFF:U_OFF].reshape(B, S, ATTN_HEADS, ATTN_V_DIM)
    u = h[..., U_OFF:GA_OFF]
    g_a = h[..., GA_OFF:GB_OFF]
    g_b = h[..., GB_OFF:IN_COLS]

    lam_init = 0.8 - 0.6 * math.exp(-0.3 * layer_idx)
    f32 = jnp.float32
    lam = (jnp.exp(jnp.sum(lam_q1.astype(f32) * lam_k1.astype(f32)))
           - jnp.exp(jnp.sum(lam_q2.astype(f32) * lam_k2.astype(f32))) + lam_init)
    o = diff_attention(q, k, v, q_gain, k_gain, lam, slopes)
    o = rmsnorm(o, head_gain) * (1.0 - lam_init)
    a_out = o.reshape(B, S, ATTN_WIDTH).astype(xn.dtype) @ w_attn_up

    s_out = s5_bidirectional(u, ssm_lam_re, ssm_lam_im, ssm_log_dt, ssm_b_re, ssm_b_im,
                             ssm_c_re, ssm_c_im, ssm_d, w_glu)
    b_out = s_out @ w_ssm_up

    merged = jax.nn.sigmoid(g_a) * a_out + jax.nn.sigmoid(g_b) * b_out
    return merged @ w_out

def hier_moe(xn, w_rg, b_rg, w_re, b_re, w1, w3, w2):
    B, S, D = xn.shape
    t = xn.reshape(B * S, D)
    T = t.shape[0]
    tf = t.astype(jnp.float32)
    g_logits = tf @ w_rg.astype(jnp.float32) + b_rg.astype(jnp.float32)
    g_prob = jax.nn.softmax(g_logits, axis=-1)
    _, g_idx = lax.top_k(g_logits, 1)
    g_w = jnp.take_along_axis(g_prob, g_idx, axis=1)[:, 0]
    e_logits = (tf @ w_re.astype(jnp.float32) + b_re.astype(jnp.float32)).reshape(
        T, N_EXPERT_GROUPS, EXPERTS_PER_GROUP)
    sel = jnp.broadcast_to(g_idx[:, :, None], (T, 1, EXPERTS_PER_GROUP))
    e_in = jnp.take_along_axis(e_logits, sel, axis=1)[:, 0]
    top_v, top_i = lax.top_k(e_in, TOP_K_INNER)
    top_w = jax.nn.softmax(top_v, axis=-1) * g_w[:, None]
    eid = g_idx * EXPERTS_PER_GROUP + top_i
    combine = jnp.sum(jax.nn.one_hot(eid, N_EXPERTS, dtype=jnp.float32)
                      * top_w[..., None], axis=1)
    out = jnp.zeros((T, D), jnp.float32)
    for e in range(N_EXPERTS):
        hid = jax.nn.silu(t @ w1[e]) * (t @ w3[e])
        out = out + combine[:, e:e + 1] * (hid @ w2[e]).astype(jnp.float32)
    return out.reshape(B, S, D).astype(xn.dtype)

def setup_inputs(seed: int = 0) -> dict:
    key = jax.random.key(seed)
    ks = iter(jax.random.split(key, 40))
    L = DEPTH
    f32 = jnp.float32

    def nrm(shape, scale):
        return scale * jax.random.normal(next(ks), shape, f32)

    x = jax.random.normal(next(ks), (BATCH, SEQ, D_MODEL), f32)
    norm1 = 1.0 + nrm((L, D_MODEL), 0.02)
    w_in = nrm((L, D_MODEL, IN_COLS), D_MODEL ** -0.5)
    q_gain = 1.0 + nrm((L, ATTN_QK_DIM), 0.02)
    k_gain = 1.0 + nrm((L, ATTN_QK_DIM), 0.02)
    lam_q1 = nrm((L, ATTN_QK_DIM), 0.1)
    lam_k1 = nrm((L, ATTN_QK_DIM), 0.1)
    lam_q2 = nrm((L, ATTN_QK_DIM), 0.1)
    lam_k2 = nrm((L, ATTN_QK_DIM), 0.1)
    head_gain = 1.0 + nrm((L, ATTN_V_DIM), 0.02)
    w_attn_up = nrm((L, ATTN_WIDTH, D_MODEL), ATTN_WIDTH ** -0.5)
    n_idx = jnp.arange(SSM_STATE, dtype=f32)
    ssm_lam_re = -0.5 + nrm((L, 2, SSM_GROUPS, SSM_STATE), 0.01)
    ssm_lam_im = jnp.pi * n_idx + nrm((L, 2, SSM_GROUPS, SSM_STATE), 0.01)
    ssm_log_dt = jax.random.uniform(next(ks), (L, 2, SSM_GROUPS), f32,
                                    minval=math.log(DT_MIN), maxval=math.log(DT_MAX))
    b_scale = (2.0 * SSM_GROUP) ** -0.5
    c_scale = (2.0 * SSM_STATE) ** -0.5
    ssm_b_re = nrm((L, 2, SSM_GROUPS, SSM_STATE, SSM_GROUP), b_scale)
    ssm_b_im = nrm((L, 2, SSM_GROUPS, SSM_STATE, SSM_GROUP), b_scale)
    ssm_c_re = nrm((L, 2, SSM_GROUPS, SSM_GROUP, SSM_STATE), c_scale)
    ssm_c_im = nrm((L, 2, SSM_GROUPS, SSM_GROUP, SSM_STATE), c_scale)
    ssm_d = nrm((L, SSM_WIDTH), 1.0)
    w_glu = nrm((L, SSM_WIDTH, SSM_WIDTH), SSM_WIDTH ** -0.5)
    w_ssm_up = nrm((L, SSM_WIDTH, D_MODEL), SSM_WIDTH ** -0.5)
    w_out = nrm((L, D_MODEL, D_MODEL), D_MODEL ** -0.5)
    norm2 = 1.0 + nrm((L, D_MODEL), 0.02)
    w_router_group = nrm((L, D_MODEL, N_EXPERT_GROUPS), D_MODEL ** -0.5)
    b_router_group = nrm((L, N_EXPERT_GROUPS), 0.01)
    w_router_expert = nrm((L, D_MODEL, N_EXPERTS), D_MODEL ** -0.5)
    b_router_expert = nrm((L, N_EXPERTS), 0.01)
    w1 = nrm((L, N_EXPERTS, D_MODEL, EXPERT_FF), D_MODEL ** -0.5)
    w3 = nrm((L, N_EXPERTS, D_MODEL, EXPERT_FF), D_MODEL ** -0.5)
    w2 = nrm((L, N_EXPERTS, EXPERT_FF, D_MODEL), EXPERT_FF ** -0.5)
    return {"x": x, "norm1": norm1, "w_in": w_in, "q_gain": q_gain, "k_gain": k_gain,
            "lam_q1": lam_q1, "lam_k1": lam_k1, "lam_q2": lam_q2, "lam_k2": lam_k2,
            "head_gain": head_gain, "w_attn_up": w_attn_up, "ssm_lam_re": ssm_lam_re,
            "ssm_lam_im": ssm_lam_im, "ssm_log_dt": ssm_log_dt, "ssm_b_re": ssm_b_re,
            "ssm_b_im": ssm_b_im, "ssm_c_re": ssm_c_re, "ssm_c_im": ssm_c_im,
            "ssm_d": ssm_d, "w_glu": w_glu, "w_ssm_up": w_ssm_up, "w_out": w_out,
            "norm2": norm2, "w_router_group": w_router_group,
            "b_router_group": b_router_group, "w_router_expert": w_router_expert,
            "b_router_expert": b_router_expert, "w1": w1, "w3": w3, "w2": w2}

def reference(x, norm1, w_in, q_gain, k_gain, lam_q1, lam_k1, lam_q2, lam_k2, head_gain,
              w_attn_up, ssm_lam_re, ssm_lam_im, ssm_log_dt, ssm_b_re, ssm_b_im,
              ssm_c_re, ssm_c_im, ssm_d, w_glu, w_ssm_up, w_out, norm2,
              w_router_group, b_router_group, w_router_expert, b_router_expert,
              w1, w3, w2):
    slopes = jnp.exp2(-8.0 * jnp.arange(1, ATTN_HEADS + 1, dtype=jnp.float32) / ATTN_HEADS)
    for l in range(DEPTH):
        xn = rmsnorm(x, norm1[l])
        x = x + hybrid_mixer(xn, l, slopes, w_in[l], q_gain[l], k_gain[l], lam_q1[l],
                             lam_k1[l], lam_q2[l], lam_k2[l], head_gain[l], w_attn_up[l],
                             ssm_lam_re[l], ssm_lam_im[l], ssm_log_dt[l], ssm_b_re[l],
                             ssm_b_im[l], ssm_c_re[l], ssm_c_im[l], ssm_d[l], w_glu[l],
                             w_ssm_up[l], w_out[l])
        xn2 = rmsnorm(x, norm2[l])
        x = x + hier_moe(xn2, w_router_group[l], b_router_group[l], w_router_expert[l],
                         b_router_expert[l], w1[l], w3[l], w2[l])
    return x


_drawn_inputs = setup_inputs


def setup_inputs(seed=0):
    import zlib

    import numpy as np

    out = dict(_drawn_inputs(seed))
    spreads = {}
    factors = {'q_gain': 3.177,
     'k_gain': 4.113,
     'lam_q1': 8.0,
     'head_gain': 3.026,
     'ssm_lam_re': 200.0,
     'ssm_log_dt': 21.736,
     'ssm_b_re': 24.632,
     'ssm_b_im': 3.0,
     'ssm_c_im': 43.168,
     'norm2': 2.86,
     'b_router_group': 8.0,
     'b_router_expert': 28.913,
     'ssm_c_re': 8.0}
    for name, (base, spread) in spreads.items():
        noise = np.random.default_rng([zlib.crc32(name.encode()), seed]).standard_normal(out[name].shape)
        drawn = base * np.exp(spread * noise) if base else spread * noise
        out[name] = __import__('jax').numpy.asarray(drawn.astype(out[name].dtype))
    for name, factor in factors.items():
        out[name] = (out[name] * factor).astype(out[name].dtype)
    return out
```

```python
import math
from contextlib import ExitStack

import concourse.bass as bass
from concourse import mybir

F32 = mybir.dt.float32
F32R = mybir.dt.float32r
I32 = mybir.dt.int32
ALU = mybir.AluOpType
ACT = mybir.ActivationFunctionType
AX_X = mybir.AxisListType.X

P = 128
D = 2048
S = 256
TT = S // P
KT = D // P
HEADS, DK, DV = 8, 64, 128
AW = HEADS * DV
SW = 1024
GRP, GP, NST = 64, 16, 64
PAIRS = GRP // 2
STEPS, CHUNKS = 8, S // 8
PC = 4
NPC = PAIRS // PC
NG, EG = 4, 4
NE, FF = NG * EG, 1024
SLOTS = 128
HALF = SLOTS // 2
EPS = 1e-6
LAM_INIT = 0.8 - 0.6 * math.exp(-0.3 * 0)
U_COL, GA_COL, GB_COL = 3 * AW, 3 * AW + SW, 3 * AW + SW + D

UW = 4 * 512
RAW, SPL = 3, 3
RAW2 = 8

BLOCKS = (
    [("w_in", U_COL + 512 * i, 4, "feat") for i in range(2)]
    + [("w_in", 512 * i, 4, "tok") for i in range(6)]
    + [("w_in", GA_COL + 512 * i, 4, "feat") for i in range(8)]
    + [("w_glu", 512 * i, 2, "feat") for i in range(2)]
    + [("w_attn_up", 512 * i, 2, "feat") for i in range(4)]
    + [("w_ssm_up", 512 * i, 2, "feat") for i in range(4)]
    + [("w_out", 512 * i, 4, "tok") for i in range(4)]
)
B_U, B_Q, B_K, B_V, B_GA, B_GB, B_GLU, B_AT, B_SS, B_OUT = 0, 2, 4, 6, 8, 12, 16, 18, 22, 26
UNITS = [(b, ku) for b, blk in enumerate(BLOCKS) for ku in range(blk[2])]
NU = len(UNITS)
LAST = [max(n for n, (b, _) in enumerate(UNITS) if b == x) for x in range(len(BLOCKS))]

LAG = 3
PREP = 2
A0 = 13
NA = 2 * NPC
QT, KTR = 33, 35
B0 = 40
H0 = 48
OT = 63

EUNITS = [(w, f, ku) for f in range(2) for w in ("w1", "w3") for ku in range(4)]
EUNITS += [("w2", 0, 0), ("w2", 1, 0), ("w2", 0, 1), ("w2", 1, 1), ("w2", 2, 0), ("w2", 2, 1), ("w2", 3, 0), ("w2", 3, 1)]
NEU = len(EUNITS)


def view(t, off, dims, p0=0, parts=P):
    row = 1
    for n in t.shape[1:]:
        row *= n
    return bass.AP(tensor=t, offset=p0 * row + off, ap=[[row, parts]] + [list(x) for x in dims])


def encoder(nc, io):
    ctx = ExitStack()
    with ctx:
        base = -(-nc.sbuf_base // 512) * 512
        room = (nc.sbuf_usable_end - base) // 32 * 32
        ctx.enter_context(nc.sbuf_tensor("arena", [P, (nc.sbuf_usable_end - nc.sbuf_base) // 4 - 16], F32))
        K1 = 1024
        OFF = dict(raw=0, hi=24 * K1, lo=48 * K1, XH=72 * K1, XL=88 * K1, GA=104 * K1, GB=120 * K1,
                   A0=136 * K1, A1=152 * K1 + 512, A2=168 * K1 + 512, A3=176 * K1 + 512,
                   A4=184 * K1 + 512, E=192 * K1 + 512, C=200 * K1 + 512)

        def at(name, region, off, shape, dt=F32):
            n = 4
            for x in shape[1:]:
                n *= x
            assert OFF[region] + off + n <= room, name
            return nc.alloc_sbuf_tensor_at(name, shape, dt, offset=base + OFF[region] + off)

        raw = at("raw", "raw", 0, [P, RAW, UW])
        whi = at("whi", "hi", 0, [P, SPL, UW], F32R)
        wlo = at("wlo", "lo", 0, [P, SPL, UW], F32R)
        x0 = at("x0", "A0", 0, [P, TT, D])
        xjunk = at("xjunk", "GB", 0, [P, TT, D])
        n1b = at("n1b", "GA", 0, [P, D])
        xh = at("xh", "XH", 0, [P, KT, S], F32R)
        xl = at("xl", "XL", 0, [P, KT, S], F32R)
        qk = at("qk", "GA", 0, [P, TT, 2 * AW])
        qT = at("qT", "GB", 0, [P, HEADS, S])
        kT = at("kT", "GB", 8 * K1, [P, HEADS, S])
        vr = at("vr", "E", 0, [P, TT, AW])
        sc = at("sc", "A2", 0, [P, 2, TT, S])
        wm = at("wm", "A2", 4 * K1, [P, TT, S])
        wT = at("wT", "A2", 6 * K1, [P, TT, S])
        orow = at("orow", "A0", 0, [P, TT, HEADS, DV])
        osq = at("osq", "E", 0, [P, TT, HEADS, DV])
        oh = at("oh", "A0", 8 * K1, [P, HEADS, S], F32R)
        ol = at("ol", "A2", 0, [P, HEADS, S], F32R)
        gA = at("gA", "GA", 0, [P, KT, S])
        gB = at("gB", "GB", 0, [P, KT, S])
        mh = at("mh", "A0", 0, [P, KT, S], F32R)
        ml = at("ml", "XL", 0, [P, KT, S], F32R)
        uT = at("uT", "A3", 0, [P, 8, S])
        U = at("U", "A3", 0, [P, GRP, CHUNKS])
        yT = at("yT", "A3", 0, [P, 8, S])
        gh = at("gh", "A1", 0, [P, 8, S], F32R)
        gl = at("gl", "A1", 8 * K1, [P, 8, S], F32R)
        sg = at("sg", "XL", 0, [P, 8, S])
        sh = at("sh", "XH", 0, [P, 8, S], F32R)
        sl = at("sl", "XH", 8 * K1, [P, 8, S], F32R)
        b_in = at("b_in", "A2", 0, [P, 2, GRP, GP])
        c_in = at("c_in", "A1", 0, [P, 2, GRP, GP])
        pw = at("pw", "A1", 8 * K1, [P, 9, 2, GRP])
        bb = at("bb", "GB", 0, [P, 2, GRP, GP])
        V = [at(f"V{d}", "GB", (8 + 4 * d) * K1, [P, 2, PC, P]) for d in range(2)]
        H = [at(f"H{d}", "A0", d * 33 * 64 * 4, [P, CHUNKS + 1, 2, PAIRS]) for d in range(2)]
        ks = [at(f"ks{d}", "A2", 4 * K1 * d, [P, GRP * GP]) for d in range(2)]
        Z = [at(f"Z{d}", "A2", 4 * K1 * d, [P, 2, PC, P]) for d in range(2)]
        Tm = at("Tm", "A4", 0, [P, 2 * PC, STEPS * GP])
        hb = at("hb", "A4", 4 * K1, [P, 2, 2, PC, 2 * CHUNKS])
        ptmp = at("ptmp", "A4", 0, [P, 2, 512])
        lag0 = at("lag0", "A4", 4 * K1, [P, GRP * GP])
        WT = at("WT", "E", 0, [P, 2, PC, P])
        vtmp = at("vtmp", "E", 4 * K1, [P, 2, 512])
        st = at("st", "E", 0, [P, 16, GRP])
        c_off = [0]

        def const(name, n, dt=F32):
            t = at(name, "C", 4 * c_off[0], [P, n], dt)
            c_off[0] += -(-n // 8) * 8
            return t

        ident = const("ident", P)
        dist = const("dist", TT * S)
        sm = const("sm", 96)
        qg, kg, hg, lam = (sm[:, i:i + 1] for i in range(4))
        rstd = sm[:, 4:6]
        nmx = sm[:, 8:12]
        den = sm[:, 12:16]
        hs_ = sm[:, 16:32]
        a8 = const("a8", 2 * 2 * PAIRS)
        rt_off = 4 * c_off[0]
        cbd = [const(f"cbd{d}", 2 * PC * 2 * GP) for d in range(2)]
        ztmp = [at("ztmp0", "A1", 12 * K1 + 512, [P, 512]), at("ztmp1", "C", 4 * (c_off[0] - 512), [P, 512])]
        dsk = const("dsk", GRP)
        lamv = at("lamv", "E", 4 * K1, [P, 4, DK])
        stepf = const("stepf", 2 * 2 * PAIRS)

        xn = at("xn", "A3", 0, [P, TT, D])
        assert OFF["A4"] - OFF["A3"] == 8 * K1

        rx = at("rx", "GA", 0, [P, 4, UW])
        re_ = at("re_", "E", 0, [P, UW])
        n2b = at("n2b", "XH", 8 * K1, [P, D])
        x2 = [at("x2a", "XH", 0, [P, D]), at("x2b", "A0", 8 * K1, [P, D])]
        xsq = at("xsq", "XH", 0, [P, TT, 2, 512])
        xnT = at("xnT", "A1", 0, [P, KT, S])
        rc = at("rc", "A2", 0, [P, 2 * P + S])
        sel = at("sel", "XL", 0, [P, TT, NE, P])
        xg = at("xg", "A0", 0, [P, D])
        sgm = at("sgm", "A0", 8 * K1, [P, 2, 512])
        hid = at("hid", "A0", 12 * K1, [P, 2, 512])
        gTh = at("gTh", "A1", 0, [P, KT, P], F32R)
        gTl = at("gTl", "A1", 8 * K1, [P, KT, P], F32R)
        hTh = at("hTh", "A2", 0, [P, 8, P], F32R)
        hTl = at("hTl", "A2", 4 * K1, [P, 8, P], F32R)
        ysb = at("ysb", "XH", 0, [P, D])
        fin = [at("fin0", "XH", 0, [P, 2, D]), at("fin1", "XL", 0, [P, 2, D])]
        NL = NG + NE
        wr = at("wr", "C", 4 * P, [P, KT, NL])
        rb = at("rb", "C", 4 * (P + KT * NL), [P, NL])
        rcs = at("rcs", "C", 4 * (P + KT * NL + NL + 4), [P, TT + NG + NE])
        n2f = at("n2f", "C", 4 * (P + KT * NL + NL + 4 + TT + NG + NE + 2), [P, KT])
        assert KT * NL + NL + 4 + TT + NG + NE + 2 + KT <= TT * S
        rt = at("rt", "C", rt_off, [P, 512])
        rc2 = at("rc2", "XH", 8 * K1, [P, P])
        wts = const("wts", 2 * TT)
        wtp = const("wtp", 2 * TT)
        ssq = const("ssq", 2 * TT * 4)
        flag = const("flag", 2, I32)
        idx = const("idx", NE, I32)
        idxc = const("idxc", 1, I32)
        held = const("held", 1)
        rows = const("rows", 2 * TT, I32)

        acc = ctx.enter_context(nc.psum_tensor("acc", [P, 4, 512], F32))
        mis = ctx.enter_context(nc.psum_tensor("mis", [P, 4, 512], F32))

        ud = nc.dram_tensor("u_scratch", [SW, S], F32).ap()
        yd = nc.dram_tensor("y_scratch", [SW, S], F32).ap()
        kd = nc.dram_tensor("lag_scratch", [GP, GRP, 2 * STEPS - 1, GP], F32).ap()

        xd = nc.dram_tensor("x2_scratch", [S, D], F32).ap()
        yr = nc.dram_tensor("expert_rows", [NE * SLOTS, D], F32).ap()
        yh = nc.dram_tensor("expert_half_rows", [NE * HALF, D], F32).ap()

        def sem(name):
            return ctx.enter_context(nc.semaphore(name))

        landed = [sem(f"unit_landed{i}") for i in range(RAW)]
        hi_ready, lo_ready, unit_used = sem("hi_ready"), sem("lo_ready"), sem("unit_used")
        acc_free = [sem(f"acc_free{i}") for i in range(2)]
        x_in = [sem(f"x_in{tt}") for tt in range(TT)]
        n1_in = sem("norm1_in")
        c_load, s_load = sem("const_in"), sem("s5_params_in")
        rms_sum, x_scaled, x_turned = sem("rms_sum"), sem("x_scaled"), sem("x_turned")
        x_hi, x_ready = sem("x_hi"), sem("x_ready")
        dve_chain, pool_chain, act_chain = sem("dve_chain"), sem("pool_chain"), sem("act_chain")
        u_stored, u_back = sem("u_stored"), sem("u_back")
        lam_sum, lam_exp = sem("lam_sum"), sem("lam_exp")
        s5_dt, s5_arg, s5_sin, pw_ready, bb_ready = (sem("s5_dt"), sem("s5_arg"), sem("s5_sin"),
                                                     sem("powers_ready"), sem("bbar_ready"))
        v_ready = [sem(f"v_ready{d}") for d in range(2)]
        v_turned, lag_done, wt_ready, in_done = sem("v_turned"), sem("lag_done"), sem("wt_ready"), sem("s5_in_done")
        s_out, k_out = sem("state_in_out"), sem("lag_out")
        lag0_in, lag0_sum, k_stored, t_in = sem("lag0_in"), sem("lag0_sum"), sem("lags_stored"), sem("t_in")
        scan_done = [sem(f"scan_done{d}") for d in range(2)]
        z_ready = [sem(f"z_ready{d}") for d in range(2)]
        hb_ready, out_done, y_out = sem("hb_ready"), sem("s5_out_done"), sem("y_out")
        y_stored, y_back, g_f, g_hi, g_ready = (sem("y_stored"), sem("y_back"), sem("gelu"), sem("g_hi"),
                                                sem("g_ready"))
        q_norm, k_norm, q_turned, q_ready = sem("q_norm"), sem("k_norm"), sem("qk_turned"), sem("qk_ready")
        sc_done, sc_out, p_ready, w_ready = sem("scores"), sem("scores_out"), sem("p_ready"), sem("w_ready")
        w_turned, wT_ready, pv_done, o_out = sem("w_turned"), sem("wT_ready"), sem("pv_done"), sem("o_out")
        o_norm, o_turned, o_hi, o_ready = sem("o_norm"), sem("o_turned"), sem("o_hi"), sem("o_ready")
        glu_s, s_hi, s_ready = sem("glu_s"), sem("s_hi"), sem("s_ready")
        merged, m_hi, m_ready = sem("merged"), sem("m_hi"), sem("m_ready")
        x_back = sem("x_back")
        landed2 = [sem(f"expert_unit_landed{i}") for i in range(RAW2)]
        r_load, ssq_out, x2_ready, x2_stored, xn_turned = (sem("router_in"), sem("ssq_out"), sem("x2_ready"),
                                                           sem("x2_stored"), sem("xn_turned"))
        x2_scaled = sem("x2_scaled")
        xnT_ready, wr_scaled, rstd_ready, logits = (sem("xnT_ready"), sem("wr_scaled"), sem("rstd_ready"),
                                                    sem("logits"))
        r_arg, r_exp, mask_ready, rank_done = sem("r_arg"), sem("r_exp"), sem("mask_ready"), sem("rank_done")
        first_split = sem("first_split")
        rc2_in, rows_ready, xg_clear = sem("overflow_slots_in"), sem("rows_ready"), sem("xg_clear")
        routed, sel_ready, idx_done, idx_ready = sem("routed"), sem("sel_ready"), sem("idx_done"), sem("idx_ready")
        held_done = sem("held_done")
        idxc_ready, xg_in, xg_turned = sem("idxc_ready"), sem("xg_in"), sem("xg_turned")
        gT_hi, gT_ready = sem("gT_hi"), sem("gT_ready")
        silu_done, hid_ready = sem("silu_done"), sem("hid_ready")
        h_turned, hT_hi, hT_ready = sem("h_turned"), sem("hT_hi"), sem("hT_ready")
        ya_out, yd_out, y_kept = sem("ya_out"), sem("yd_out"), sem("y_kept")
        fin_in = [sem(f"fin_in{i}") for i in range(TT)]
        fin_done, stored = sem("fin_done"), sem("stored")

        def slot(u):
            return rx[:, u] if u < 4 else re_[:] if u == 4 else raw[:, (u - 4) % RAW]
        assert (NU - 1) % RAW == 0 and RAW2 == 5 + RAW

        GB_OF = [3, 2, 2, 3]

        def overflow(eng, body):
            more = eng.value_load(flag[0:1, 0:1], min_val=0, max_val=1)
            with eng.If(more > 0):
                body()
                eng.nop()

        def chain(eng, s):
            n = [0]

            def link(ins):
                n[0] += 1
                ins.then_inc(s, 1)
                eng.wait_ge(s, n[0])
            counts = {}

            def own(s, value=None):
                counts[s.name] = value or counts.get(s.name, 0) + 1
                eng.wait_ge(s, counts[s.name])
            link.own = own
            return link

        def evacuated(eng, b):
            eng.wait_ge(acc_free[b % 2], b // 2 + 1)

        def acc_of(b):
            return view(acc, 1024 * (b % 2), [[1, 1024]])

        def cmul(e, link, out_re, out_im, a_re, a_im, b_re, b_im, tmp, neg=False):
            link(e.tensor_tensor(out_re, a_re, b_re, ALU.mult))
            link(e.tensor_tensor(tmp, a_im, b_im, ALU.mult))
            link(e.tensor_tensor(out_re, out_re, tmp, ALU.add if neg else ALU.subtract))
            link(e.tensor_tensor(out_im, a_re, b_im, ALU.mult))
            link(e.tensor_tensor(tmp, a_im, b_re, ALU.mult))
            return e.tensor_tensor(out_im, out_im, tmp, ALU.subtract if neg else ALU.add)

        def v_build(e, link, i, tmp):
            d, ch = i % 2, i // 2
            dj = d * PAIRS + PC * ch

            def powers(ri):
                k0, dk = (7, -1) if d == 0 else (0, 1)
                return view(pw, (k0 * 2 + ri) * GRP + dj, [[1, PC], [dk * 2 * GRP, STEPS], [0, GP]])

            def coef(ri):
                return view(bb, ri * GRP * GP + dj * GP, [[GP, PC], [0, STEPS], [1, GP]])

            def out(ri):
                return view(V[d], ri * PC * P, [[P, PC], [GP, STEPS], [1, GP]])
            t0 = view(tmp, 0, [[P, PC], [GP, STEPS], [1, GP]])
            for g2 in range(2):
                link(e.tensor_copy(
                    view(cbd[d], g2 * GP, [[PC * 2 * GP, 2], [2 * GP, PC], [1, GP]], 64 * g2, 64),
                    view(c_in, dj * GP, [[GRP * GP, 2], [GP, PC], [1, GP]], 64 * g2, 64)))
            cmul(e, link, out(0), out(1), powers(0), powers(1), coef(0), coef(1), t0
                 ).then_inc(v_ready[d], 1)
            link.own(v_ready[d])

        def z_build(e, link, d, ch, tmp):
            dj = d * PAIRS + PC * ch

            def powers(ri):
                k0, dk = (1, 1) if d == 0 else (8, -1)
                return view(pw, (k0 * 2 + ri) * GRP + dj, [[1, PC], [dk * 2 * GRP, STEPS], [0, GP]])

            def coef(ri):
                return view(c_in, ri * GRP * GP + dj * GP, [[GP, PC], [0, STEPS], [1, GP]])

            def out(ri):
                return view(Z[d], ri * PC * P, [[P, PC], [GP, STEPS], [1, GP]])
            t0 = view(tmp, 0, [[P, PC], [GP, STEPS], [1, GP]])
            cmul(e, link, out(0), out(1), powers(0), powers(1), coef(0), coef(1), t0, neg=True
                 ).then_inc(z_ready[d], 1)
            link.own(z_ready[d])

        def scan_steps(e, link, d, tmp, i0, i1):
            ar = view(pw, 16 * GRP + d * PAIRS, [[0, 2], [1, PAIRS]])
            ai = view(a8, d * 2 * PAIRS, [[PAIRS, 2], [1, PAIRS]])
            t0, t1 = (view(tmp, 2 * PAIRS * k, [[PAIRS, 2], [1, PAIRS]]) for k in range(2))
            for i in range(i0, i1):
                cur = view(H[d], 64 * (i + 1), [[PAIRS, 2], [1, PAIRS]])
                link(e.tensor_tensor(t0, ar, view(H[d], 64 * i, [[PAIRS, 2], [1, PAIRS]]), ALU.mult))
                link(e.tensor_tensor(t1, ai, view(H[d], 64 * i + PAIRS, [[-PAIRS, 2], [1, PAIRS]]), ALU.mult))
                link(e.tensor_tensor(cur, cur, t0, ALU.add))
                last = e.tensor_tensor(cur, cur, t1, ALU.add)
                if i == CHUNKS - 1:
                    last.then_inc(scan_done[d], 1)
                    link.own(scan_done[d])
                else:
                    link(last)

        block = ctx.enter_context(nc.Block())

        @block.sync
        def _(sp):
            for tt in range(TT):
                sp.dma_start(x0[:, tt], io["x"][tt * P:(tt + 1) * P]).then_inc(x_in[tt], 16)
                if tt == 0:
                    sp.dma_start(ident[:], io["ident"]).then_inc(c_load, 16)
                    sp.dma_start(n1b[:], io["norm1"].broadcast_to([P, D])).then_inc(n1_in, 16)
            for n, (b, ku) in enumerate(UNITS):
                w, col, _, _ = BLOCKS[b]
                if n >= RAW:
                    sp.wait_ge(lo_ready, n - RAW + 1)
                src = io[w][ku * 512:(ku + 1) * 512, col:col + 512].rearrange("(i p) c -> p i c", p=P)
                sp.dma_start(raw[:, n % RAW].rearrange("p (i c) -> p i c", i=4), src
                             ).then_inc(landed[n % RAW], 16)
                if n == 2:
                    sp.dma_start(st[:, 0], io["lam_re"]).then_inc(s_load, 16)
                    sp.dma_start(st[:, 1], io["lam_im"]).then_inc(s_load, 16)
                    for g2 in range(2):
                        sp.dma_start(st[64 * g2:64 * g2 + 64, 2], io["log_dt"][g2:g2 + 1, :].broadcast_to([64, GRP])
                                     ).then_inc(s_load, 16)
                    for ri in range(2):
                        sp.dma_start(b_in[:, ri], io["b"][ri]).then_inc(s_load, 16)
                        sp.dma_start(c_in[:, ri], io["c"][ri]).then_inc(s_load, 16)
                    sp.dma_start(dist[:], io["dist"]).then_inc(s_load, 16)
                    for s in range(STEPS):
                        sp.dma_start(dsk[GP * s:GP * s + GP], io["d_skip"]).then_inc(s_load, 16)
                    for h2 in range(2):
                        sp.dma_start(sm[64 * h2:64 * h2 + 64, 0:1], io["q_gain"]).then_inc(s_load, 16)
                        sp.dma_start(sm[64 * h2:64 * h2 + 64, 1:2], io["k_gain"]).then_inc(s_load, 16)
                    sp.dma_start(sm[:, 2:3], io["head_gain"]).then_inc(s_load, 16)
                    for i, v in enumerate(("lam_q1", "lam_k1", "lam_q2", "lam_k2")):
                        sp.dma_start(lamv[:, i], io[v].broadcast_to([P, DK])).then_inc(s_load, 16)
                ch = n - B0 - 2
                if 0 <= ch < NPC:
                    if ch == 0:
                        sp.wait_ge(k_stored, 16 * 15)
                        sp.wait_ge(scan_done[1], 1)
                    else:
                        sp.wait_ge(out_done, ch)
                    for s in range(STEPS):
                        sp.dma_start(Tm[GP * s:GP * s + GP],
                                     kd[:, 2 * PC * ch:2 * PC * (ch + 1), 7 - s:15 - s].rearrange("p g m q -> p g (m q)")
                                     ).then_inc(t_in, 16)
                if n == H0 + 4:
                    sp.wait_ge(y_out, NPC)
                    for s in range(STEPS):
                        sp.dma_start(yd.rearrange("(g p) (s c) -> s p g c", p=GP, s=STEPS)[s],
                                     U[GP * s:GP * s + GP]).then_inc(y_stored, 16)
                if n == H0 + 6:
                    sp.wait_ge(y_stored, 16 * STEPS)
                    sp.dma_start(yT[:], yd.rearrange("(f p) t -> p f t", p=P)).then_inc(y_back, 16)
                if n == LAST[B_SS + 3] + 6:
                    sp.wait_ge(unit_used, LAST[B_SS + 3] + 1)
                    sp.dma_start(n2b[:], io["norm2"].broadcast_to([P, D])).then_inc(r_load, 16)
                    sp.dma_start(rc[:], io["router_tables"]).then_inc(r_load, 16)
                    sp.dma_start(wr[:], io["w_router"]).then_inc(r_load, 16)
                    sp.dma_start(rb[:], io["b_router"].broadcast_to([P, NL])).then_inc(r_load, 16)
                    sp.dma_start(rcs[:], io["router_rows"]).then_inc(r_load, 16)
                    sp.dma_start(n2f[:], io["norm2_features"]).then_inc(r_load, 16)
                if n == LAST[B_GLU + 1] + 7:
                    sp.wait_ge(s_ready, 2)
                    for tt in range(TT):
                        sp.dma_start(xn[:, tt], io["x"][tt * P:(tt + 1) * P]).then_inc(x_back, 16)

            def experts(p):
                base = NU + p * NE * NEU
                if p:
                    sp.wait_ge(fin_done, TT)
                    sp.dma_start(rc2[:], io["router_tables"][:, 3 * P:4 * P]).then_inc(rc2_in, 16)
                with sp.Fori(0, NE) as e:
                    for u, (w, c, ku) in enumerate(EUNITS):
                        sp.wait_ge(lo_ready, e * NEU + (base + u - RAW2 + 1))
                        src = io[w][bass.ds(e, 1), ku * 512:(ku + 1) * 512, c * 512:c * 512 + 512]
                        sp.dma_start(slot(u % RAW2).rearrange("p (i c) -> p i c", i=4),
                                     src.rearrange("o (i p) c -> p (o i) c", p=P)).then_inc(landed2[u % RAW2], 16)

            sp.wait_ge(m_ready, 4)
            experts(0)
            sp.wait_ge(routed, 1)

            def again():
                experts(1)
                sp.wait_ge(fin_done, 2 * TT)
            overflow(sp, again)
            for tt in range(TT):
                sp.wait_ge(fin_done, tt + 1)
                sp.dma_start(io["out"][tt * P:(tt + 1) * P], xn[:, tt]).then_inc(stored, 16)
            sp.wait_ge(stored, 16 * TT)

        N_SLOAD = 4 + 4 + 1 + STEPS + 4 + 1 + 4

        @block.tensor
        def _(pe):
            mm = nc.tensor.matmul

            def three(out, a_hi, a_lo, b_hi, b_lo, start, stop):
                mm(out, a_hi, b_hi, start=start, stop=False, skip_group_check=True)
                mm(out, a_hi, b_lo, start=False, stop=False, skip_group_check=True)
                return mm(out, a_lo, b_hi, start=False, stop=stop, skip_group_check=True)

            def turn_new_x(f):
                evacuated(pe, B_OUT + f)
                if f:
                    pe.wait_ge(xnT_ready, f)
                for k in range(4):
                    for tt in range(TT):
                        ins = nc.tensor.transpose(view(mis, k * S + tt * P, [[1, P]]),
                                                  xn[:, tt, (4 * f + k) * P:(4 * f + k + 1) * P], ident[:])
                ins.then_inc(xn_turned, 1)

            def router_logits(f):
                pe.wait_ge(xnT_ready, f + 1)
                if f == 0:
                    pe.wait_ge(wr_scaled, 1)
                for k in range(4 * f, 4 * f + 4):
                    for tt in range(TT):
                        ins = mm(view(mis, 1024 + 32 * tt, [[1, NL]]), xnT[:, k, tt * P:(tt + 1) * P], wr[:, k],
                                 start=k == 0 and tt == 0, stop=k == KT - 1, skip_group_check=True)
                if f == 3:
                    ins.then_inc(logits, 1)

            pe.wait_ge(c_load, 16)
            for tt in range(TT):
                pe.wait_ge(x_scaled, tt + 1)
                bank = mis if tt == 0 else acc
                for k in range(KT):
                    ins = nc.tensor.transpose(view(bank, k * P, [[1, P]]), x0[:, tt, k * P:(k + 1) * P], ident[:])
                ins.then_inc(x_turned, 1)
            pe.wait_ge(x_ready, TT)

            halves = {B_GLU: (gh, gl), B_AT: (oh, ol), B_SS: (sh, sl), B_OUT: (mh, ml)}
            for n, (b, ku) in enumerate(UNITS):
                _, _, nku, layout = BLOCKS[b]
                if ku == 0 and b >= 2:
                    pe.wait_ge(acc_free[b % 2], b // 2)
                if n == 0:
                    act_h, act_l = xh, xl
                if b in halves and ku == 0:
                    act_h, act_l = halves[b]
                if b == B_GLU and ku == 0:
                    pe.wait_ge(g_ready, 1)
                if b == B_AT and ku == 0:
                    pe.wait_ge(o_ready, 1)
                if b == B_SS:
                    pe.wait_ge(s_ready, ku + 1)
                if b == B_OUT:
                    pe.wait_ge(m_ready, ku + 1)
                pe.wait_ge(lo_ready, n + 1)
                r = n % SPL
                for i in range(4):
                    k = 4 * ku + i
                    first, last = ku == 0 and i == 0, ku == nku - 1 and i == 3
                    for m in range(4 if layout == "feat" else TT):
                        if layout == "feat":
                            w = [t[:, r, 512 * i + P * m:512 * i + P * m + P] for t in (whi, wlo)]
                            out = view(acc, 1024 * (b % 2) + S * m, [[1, S]])
                            ins = three(out, w[0], w[1], act_h[:, k], act_l[:, k], first and m % 2 == 0, last)
                        else:
                            a = [t[:, k, P * m:P * m + P] for t in (act_h, act_l)]
                            w = [t[:, r, 512 * i:512 * i + 512] for t in (whi, wlo)]
                            ins = three(acc[:, 2 * (b % 2) + m], a[0], a[1], w[0], w[1], first, last)
                ins.then_inc(unit_used, 1)

                i = n - A0 - 1
                if 0 <= i < NA:
                    d, ch = i % 2, i // 2
                    pe.wait_ge(wt_ready, i + 1)
                    if i == 0:
                        pe.wait_ge(u_back, 16 * STEPS)
                    else:
                        pe.wait_ge(s_out, i)
                    for j in range(PC):
                        for ri in range(2):
                            ins = mm(view(mis, 1024 + (2 * j + ri) * 64, [[1, 64]]), WT[:, ri, j],
                                     view(U, 2 * (PC * ch + j) * CHUNKS, [[1, 64]]), start=True, stop=True)
                    ins.then_inc(in_done, 1)
                i = n - A0
                if 0 <= i < NA:
                    d, ch = i % 2, i // 2
                    pe.wait_ge(v_ready[d], ch + 1)
                    if i:
                        pe.wait_ge(wt_ready, i)
                    for ri in range(2):
                        for j in range(PC):
                            ins = nc.tensor.transpose(view(mis, (ri * PC + j) * P, [[1, P]]), V[d][:, ri, j], ident[:])
                    ins.then_inc(v_turned, 1)
                    if i:
                        pe.wait_ge(k_out, i)
                    for j in range(PC):
                        for ri in range(2):
                            ins = mm(view(mis, 1536 + 32 * j, [[1, 32]]), V[d][:, ri, j],
                                     view(cbd[d], (ri * PC + j) * 32, [[1, 32]]), start=ri == 0, stop=ri == 1)
                    ins.then_inc(lag_done, 1)
                if n in (QT, KTR):
                    half = int(n == KTR)
                    pe.wait_ge([q_norm, k_norm][half], TT)
                    if half:
                        pe.wait_ge(q_ready, 1)
                    else:
                        pe.wait_ge(s_out, NA)
                        pe.wait_ge(k_out, NA)
                    for h in range(HEADS):
                        for tt in range(TT):
                            ins = nc.tensor.transpose(view(mis, h * S + tt * P, [[1, P]]),
                                                      qk[:, tt, half * AW + h * P:half * AW + (h + 1) * P], ident[:])
                    ins.then_inc(q_turned, 1)
                ch = n - B0
                if 0 <= ch < NPC:
                    pe.wait_ge(t_in, 16 * STEPS * (ch + 1))
                    pe.wait_ge(hb_ready, ch + 1)
                    for d in range(2):
                        pe.wait_ge(z_ready[d], ch + 1)
                    if ch == 0:
                        pe.wait_ge(q_ready, 2)
                    if ch >= 2:
                        pe.wait_ge(y_out, ch - 1)
                    bank = 512 * (ch % 2)
                    for g in range(2 * PC):
                        mm(view(mis, bank + 32 * g, [[1, 32]]), Tm[:, g],
                           U[:, 2 * PC * ch + g], start=g == 0, stop=False, skip_group_check=True)
                    for j in range(PC):
                        for d in range(2):
                            for ri in range(2):
                                ins = mm(view(mis, bank + 64 * j, [[1, 64]]), Z[d][:, ri, j], hb[:, ri, d, j],
                                         start=False, stop=d == 1 and ri == 1, skip_group_check=True)
                    ins.then_inc(out_done, 1)
                h = n - H0 - 3
                if 0 <= h < HEADS:
                    pe.wait_ge(wT_ready, h + 1)
                    if h:
                        pe.wait_ge(o_out, h)
                    for qt in range(TT):
                        for kt in range(TT):
                            ins = mm(view(mis, 1536 + qt * P, [[1, P]]), view(wT, kt * S + qt * P, [[1, P]]),
                                     vr[:, kt, h * DV:(h + 1) * DV], start=kt == 0, stop=kt == 1)
                    ins.then_inc(pv_done, 1)
                h = n - H0 - 2
                if 0 <= h < HEADS:
                    pe.wait_ge(w_ready, h + 1)
                    if h:
                        pe.wait_ge(wT_ready, h)
                    for kt in range(TT):
                        for qt in range(TT):
                            ins = nc.tensor.transpose(view(mis, 1024 + kt * S + qt * P, [[1, P]]),
                                                      wm[:, qt, kt * P:(kt + 1) * P], ident[:])
                    ins.then_inc(w_turned, 1)
                h = n - H0
                if 0 <= h < HEADS:
                    if h:
                        pe.wait_ge(sc_out, h)
                    else:
                        pe.wait_ge(y_out, NPC)
                    for m in range(2):
                        for qt in range(TT):
                            ins = mm(view(mis, 512 * m + S * qt, [[1, S]]),
                                     view(qT, h * S + qt * P, [[1, P]], 64 * m, 64),
                                     view(kT, h * S, [[1, S]], 64 * m, 64), start=True, stop=True)
                    ins.then_inc(sc_done, 1)
                for f in range(3):
                    if n == LAST[B_OUT + f] + 1:
                        turn_new_x(f)
                    if n == LAST[B_OUT + f] + 3:
                        router_logits(f)
                if n == OT:
                    pe.wait_ge(o_norm, 1)
                    for h in range(HEADS):
                        for tt in range(TT):
                            ins = nc.tensor.transpose(view(mis, h * S + tt * P, [[1, P]]), orow[:, tt, h], ident[:])
                    ins.then_inc(o_turned, 1)

            turn_new_x(3)
            router_logits(3)
            pe.wait_ge(mask_ready, 1)
            for tt in range(TT):
                if tt:
                    mm(view(mis, 512 + NE * tt, [[1, NE]]), rc[:, P:2 * P], view(rt, 0, [[1, NE]]),
                       start=True, stop=False, skip_group_check=True)
                mm(view(mis, 512 + NE * tt, [[1, NE]]), rc[:, 0:P], view(rt, NE * tt, [[1, NE]]),
                   start=tt == 0, stop=True, skip_group_check=True)
            for tt in range(TT):
                ins = mm(view(mis, 512 + NE * 2, [[1, NE]]), rc[:, P:2 * P], view(rt, NE * tt, [[1, NE]]),
                         start=tt == 0, stop=tt == 1, skip_group_check=True)
            ins.then_inc(rank_done, 1)

            def experts(p):
                base, q = NU + p * NE * NEU, p * NE
                pe.wait_ge(sel_ready, p + 1)
                for e in range(NE):
                    for tt in range(TT):
                        ins = mm(view(mis, (0 if e else 1024) + e, [[1, 1]]), sel[:, tt, e], rcs[:, tt:tt + 1],
                                 start=tt == 0, stop=tt == 1)
                    if e in (0, NE - 1):
                        ins.then_inc(idx_done, 1)

                def turn_rows(e, b):
                    for k in range(4):
                        ins = nc.tensor.transpose(view(mis, GB_OF[b] * 512 + k * P, [[1, P]]),
                                                  xg[:, (4 * b + k) * P:(4 * b + k + 1) * P], ident[:])
                    ins.then_inc(xg_turned, 1)

                def turn_hidden(e, f):
                    pe.wait_ge(hid_ready, e * 2 + (2 * q + f + 1))
                    for k in range(4):
                        ins = nc.tensor.transpose(view(mis, (2 + f) * 512 + k * P, [[1, P]]),
                                                  hid[:, f, k * P:(k + 1) * P], ident[:])
                    ins.then_inc(h_turned, 1)

                def body(e, last):
                    for u, (w, c, ku) in enumerate(EUNITS):
                        if u == 0:
                            pe.wait_ge(gT_ready, e * 4 + (4 * q + 4))
                        if u == 16:
                            pe.wait_ge(hT_ready, e * 2 + (2 * q + 1))
                            pe.wait_ge(ya_out, e * 2 + (2 * q + 1))
                        if u == 17:
                            pe.wait_ge(yd_out, e * 2 + (2 * q + 1))
                        if u == 18:
                            pe.wait_ge(hT_ready, e * 2 + (2 * q + 2))
                        if u == 20:
                            pe.wait_ge(ya_out, e * 2 + (2 * q + 2))
                        if u == 22:
                            pe.wait_ge(yd_out, e * 2 + (2 * q + 2))
                        pe.wait_ge(lo_ready, e * NEU + (base + u + 1))
                        r = (base + u) % SPL
                        for i in range(4):
                            k = 4 * ku + i
                            wh, wl = (t[:, r, 512 * i:512 * i + 512] for t in (whi, wlo))
                            if w == "w2":
                                out, ah, al, nk = mis[:, c % 2], hTh[:, k], hTl[:, k], 8
                            else:
                                out, ah, al, nk = acc[:, 2 * c + (w == "w3")], gTh[:, k], gTl[:, k], 16
                            ins = three(out, ah, al, wh, wl, k == 0, k == nk - 1)
                        ins.then_inc(unit_used, 1)
                        if u == 11:
                            turn_hidden(e, 0)
                        if u == 15 and not last:
                            pe.wait_ge(xg_in, e * 16 + 16 * (q + 2))
                            turn_rows(e, 0)
                            pe.wait_ge(hT_ready, e * 2 + (2 * q + 1))
                            turn_rows(e, 1)
                        if u == 16:
                            if not last:
                                pe.wait_ge(gT_ready, e * 4 + (4 * q + 5))
                            turn_hidden(e, 1)
                        if u == 17 and not last:
                            pe.wait_ge(gT_ready, e * 4 + (4 * q + 6))
                            turn_rows(e, 2)
                            pe.wait_ge(hT_ready, e * 2 + (2 * q + 2))
                            turn_rows(e, 3)

                pe.wait_ge(xg_in, 16 * (q + 1))
                for b in range(4):
                    if b >= 2:
                        pe.wait_ge(gT_ready, 4 * q + (2 if b == 2 else 1))
                    turn_rows(0, b)
                with pe.Fori(0, NE - 1) as e:
                    body(e, False)
                body(NE - 1, True)

            experts(0)
            overflow(pe, lambda: experts(1))

        @block.scalar
        def _(act):
            a = nc.scalar.activation
            own = chain(act, act_chain).own
            for tt in range(TT):
                act.wait_ge(x_in[tt], 16)
                a(xjunk[:, tt], x0[:, tt], ACT.Square, accum_out=rstd[:, tt:tt + 1]).then_inc(rms_sum, 1)
                own(rms_sum)
            for tt in range(TT):
                act.wait_ge(x_turned, tt + 1)
                a(view(xh, tt * P, [[S, KT], [1, P]]), view(mis if tt == 0 else acc, 0, [[P, KT], [1, P]]), ACT.Copy
                  ).then_inc(x_hi, 1)
                own(x_hi)

            def hi(n):
                act.wait_ge(landed[n % RAW], 16 * (n // RAW + 1))
                if n >= SPL:
                    act.wait_ge(unit_used, n - SPL + 1)
                a(whi[:, n % SPL], raw[:, n % RAW], ACT.Copy).then_inc(hi_ready, 1)
                own(hi_ready)

            for n in range(NU + 4):
                if n < NU:
                    hi(n)
                if n == PREP:
                    act.wait_ge(s_load, 16 * N_SLOAD)
                    a(st[:, 2], st[:, 2], ACT.Exp).then_inc(s5_dt, 1)
                    own(s5_dt)
                if n == PREP + 2:
                    act.wait_ge(lam_sum, 1)
                    a(sm[:, 34:36], sm[:, 32:34], ACT.Exp).then_inc(lam_exp, 1)
                    own(lam_exp)
                    act.wait_ge(s5_arg, 1)
                    a(st[:, 3], st[:, 3], ACT.Exp).then_inc(s5_sin, 1)
                    own(s5_sin)
                    a(st[:, 5], st[:, 4], ACT.Sin).then_inc(s5_sin, 1)
                    own(s5_sin)
                    a(st[:, 6], st[:, 4], ACT.Sin, scale=0.5).then_inc(s5_sin, 1)
                    own(s5_sin)
                for b in range(len(BLOCKS)):
                    if n != {B_V: A0 + NA + LAG + 1, B_GB: H0 + HEADS - 1 + LAG}.get(b, LAST[b] + LAG):
                        continue
                    if b < B_Q or B_V <= b < B_GLU + 2:
                        act.wait_ge(unit_used, LAST[b] + 1)
                    if b < B_Q:
                        a(uT[:, 4 * b:4 * b + 4], acc_of(b), ACT.Copy).then_inc(acc_free[b % 2], 1)
                        own(acc_free[b % 2], b // 2 + 1)
                    elif B_V <= b < B_GA:
                        if b == B_V:
                            act.wait_ge(in_done, NA)
                            act.wait_ge(v_ready[0], NPC)
                        a(vr[:, :, 512 * (b - B_V):512 * (b - B_V) + 512], acc_of(b), ACT.Copy
                          ).then_inc(acc_free[b % 2], 1)
                        own(acc_free[b % 2], b // 2 + 1)
                    elif B_GA <= b < B_GLU:
                        if b == B_GA:
                            act.wait_ge(q_turned, 2)
                        if b == B_GB:
                            act.wait_ge(sc_done, HEADS)
                        g, f = (gA, b - B_GA) if b < B_GB else (gB, b - B_GB)
                        a(g[:, 4 * f:4 * f + 4], acc_of(b), ACT.Sigmoid).then_inc(acc_free[b % 2], 1)
                        own(acc_free[b % 2], b // 2 + 1)
                    elif B_GLU <= b < B_AT:
                        f = b - B_GLU
                        a(sg[:, 4 * f:4 * f + 4], acc_of(b), ACT.Sigmoid).then_inc(acc_free[b % 2], 1)
                        own(acc_free[b % 2], b // 2 + 1)
                if n in (LAST[0] + LAG, LAST[1] + LAG):
                    b = int(n == LAST[1] + LAG)
                    evacuated(act, b)
                    act.dma_start(ud.rearrange("(f p) t -> p f t", p=P)[:, 4 * b:4 * b + 4],
                                  uT[:, 4 * b:4 * b + 4]).then_inc(u_stored, 16)
                if n == LAST[1] + LAG + 1:
                    act.wait_ge(u_stored, 32)
                    for s in range(STEPS):
                        act.dma_start(U[GP * s:GP * s + GP],
                                      ud.rearrange("(g p) (s c) -> s p g c", p=GP, s=STEPS)[s]).then_inc(u_back, 16)
                i = n - A0 - LAG
                if 0 <= i < NA:
                    act.wait_ge(v_turned, i + 1)
                    if i == 0:
                        act.wait_ge(pw_ready, 1)
                        act.wait_ge(bb_ready, 1)
                    a(WT[:], view(mis, 0, [[1, 1024]]), ACT.Copy).then_inc(wt_ready, 1)
                    own(wt_ready)
                    act.wait_ge(lag_done, i + 1)
                    a(ks[i % 2][:, 128 * (i // 2):128 * (i // 2) + 128], view(mis, 1536, [[1, 128]]), ACT.Copy
                      ).then_inc(k_out, 1)
                    own(k_out)
                if n == A0 + NA + LAG + 1:
                    act.wait_ge(k_out, NA)
                    act.wait_ge(v_ready[1], NPC)
                    act.dma_start(lag0[112:128], ks[1][0:GP]).then_inc(lag0_in, 16)
                if n == A0 + NA + LAG + 3:
                    act.wait_ge(lag0_sum, 1)
                    for s in range(STEPS):
                        act.dma_start(kd[:, :, 14 - s], ks[0][GP * s:GP * s + GP].rearrange("p (g q) -> p g q", q=GP)).then_inc(k_stored, 16)
                    for s in range(1, STEPS):
                        act.dma_start(kd[:, :, 7 - s], ks[1][GP * s:GP * s + GP].rearrange("p (g q) -> p g q", q=GP)).then_inc(k_stored, 16)
                if n in (QT + LAG, KTR + LAG):
                    half = int(n == KTR + LAG)
                    act.wait_ge(q_turned, half + 1)
                    if not half:
                        act.wait_ge(in_done, NA)
                    a((kT if half else qT)[:], view(mis, 0, [[1, 2048]]), ACT.Copy, scale=kg if half else qg
                      ).then_inc(q_ready, 1)
                    own(q_ready)
                ch = n - B0 - LAG + 1
                if 0 <= ch < NPC:
                    if ch == 0:
                        act.wait_ge(lag0_sum, 2)
                        act.wait_ge(scan_done[0], 1)
                        act.wait_ge(scan_done[1], 1)
                    else:
                        act.wait_ge(out_done, ch)
                    for d in range(2):
                        for g2 in range(2):
                            ins = a(view(hb, d * 256 + g2 * 32, [[512, 2], [64, PC], [1, CHUNKS]], 64 * g2, 64),
                                    view(H[d], PC * ch + (0 if d == 0 else 31 * 64),
                                         [[PAIRS, 2], [1, PC], [64 if d == 0 else -64, CHUNKS]], 64 * g2, 64), ACT.Copy)
                    ins.then_inc(hb_ready, 1)
                    own(hb_ready)
                h = n - H0 - 3 - LAG
                if 0 <= h < HEADS:
                    act.wait_ge(pv_done, h + 1)
                    if h == 0:
                        act.wait_ge(hb_ready, NPC)
                    a(orow[:, :, h], view(mis, 1536, [[1, 256]]), ACT.Copy).then_inc(o_out, 1)
                    own(o_out)
                h = n - H0 - 2 - LAG
                if 0 <= h < HEADS:
                    act.wait_ge(w_turned, h + 1)
                    if h:
                        act.wait_ge(pv_done, h)
                    a(wT[:], view(mis, 1024, [[1, 512]]), ACT.Copy).then_inc(wT_ready, 1)
                    own(wT_ready)
                h = n - H0 - LAG
                if 0 <= h < HEADS:
                    act.wait_ge(sc_out, h + 1)
                    for m in range(2):
                        for qt in range(TT):
                            i = 2 * m + qt
                            ins = a(sc[:, m, qt], sc[:, m, qt], ACT.Exp, bias=nmx[:, i:i + 1],
                                    accum_out=den[:, i:i + 1])
                            ins.then_inc(p_ready, 1)
                            own(p_ready)
                if n == H0 + 12:
                    act.wait_ge(y_back, 16)
                    act.wait_ge(y_out, NPC)
                    act.wait_ge(z_ready[1], NPC)
                    a(yT[:], yT[:], ACT.Gelu_apprx_tanh).then_inc(g_f, 1)
                    own(g_f)
                    act.wait_ge(g_f, 1)
                    a(gh[:], yT[:], ACT.Copy).then_inc(g_hi, 1)
                    own(g_hi)
                if n == OT + LAG:
                    act.wait_ge(o_turned, 1)
                    a(oh[:], view(mis, 0, [[1, 2048]]), ACT.Copy, scale=hg).then_inc(o_hi, 1)
                    own(o_hi)
                for f in range(2):
                    if n == LAST[B_GLU + f] + LAG + 1:
                        act.wait_ge(glu_s, f + 1)
                        a(sh[:, 4 * f:4 * f + 4], yT[:, 4 * f:4 * f + 4], ACT.Copy).then_inc(s_hi, 1)
                        own(s_hi)
                for f in range(4):
                    if n == LAST[B_OUT + f] + LAG:
                        evacuated(act, B_OUT + f)
                        if f >= 2:
                            act.wait_ge(ssq_out, 2 * (f - 1))
                        for tt in range(TT):
                            a(xsq[:, tt, f % 2], xn[:, tt, 512 * f:512 * f + 512], ACT.Square,
                              accum_out=ssq[:, 4 * tt + f:4 * tt + f + 1]).then_inc(ssq_out, 1)
                    if n == LAST[B_OUT + f] + LAG + (1 if f < 3 else 0):
                        act.wait_ge(xn_turned, f + 1)
                        a(xnT[:, 4 * f:4 * f + 4], view(mis, 0, [[1, 4 * S]]), ACT.Copy).then_inc(xnT_ready, 1)
                    if n == LAST[B_SS + f] + LAG:
                        act.wait_ge(merged, f + 1)
                        a(mh[:, 4 * f:4 * f + 4], gB[:, 4 * f:4 * f + 4], ACT.Copy).then_inc(m_hi, 1)
                        own(m_hi)

            act.wait_ge(rstd_ready, 1)
            act.wait_ge(unit_used, NU)
            act.wait_ge(ssq_out, 2 * 4)
            for tt in range(TT):
                a(x2[tt][:], xn[:, tt], ACT.Copy, scale=rstd[:, tt:tt + 1]).then_inc(x2_scaled, 1)
            for i in range(2):
                act.wait_ge(r_arg, i + 1)
                z = view(rt, 64, [[1, TT * NG]]) if i == 0 else view(rt, 80, [[1, TT]])
                a(z, z, ACT.Exp).then_inc(r_exp, 1)

            act.nop().then_inc(ya_out, 1)

            def experts(p):
                base, q = NU + p * NE * NEU, p * NE

                def hi2(e, u):
                    act.wait_ge(landed2[u % RAW2], e * (16 * 3) + 16 * (3 * q + u // RAW2 + 1))
                    act.wait_ge(unit_used, e * NEU + (base + u - SPL + 1))
                    a(whi[:, (base + u) % SPL], slot(u % RAW2), ACT.Copy).then_inc(hi_ready, 1)

                def rows_hi(e, b):
                    act.wait_ge(xg_turned, e * 4 + (4 * q + b + 1))
                    a(gTh[:, 4 * b:4 * b + 4], mis[:, GB_OF[b]].rearrange("p (k t) -> p k t", t=P), ACT.Copy
                      ).then_inc(gT_hi, 1)

                def hidden_hi(e, f):
                    act.wait_ge(h_turned, e * 2 + (2 * q + f + 1))
                    a(hTh[:, 4 * f:4 * f + 4], mis[:, 2 + f].rearrange("p (k t) -> p k t", t=P), ACT.Copy
                      ).then_inc(hT_hi, 1)

                def body(e, last):
                    for u in range(NEU):
                        if u + SPL < NEU:
                            hi2(e, u + SPL)
                        elif not last:
                            hi2(e + 1, u + SPL - NEU)
                        if u in (7, 15):
                            f = u // 8
                            act.wait_ge(unit_used, e * NEU + (base + u + 1))
                            a(sgm[:, f], acc[:, 2 * f], ACT.Silu).then_inc(silu_done, 1)
                        if u == 11:
                            hidden_hi(e, 0)
                        if u == 15 and not last:
                            rows_hi(e + 1, 0)
                            rows_hi(e + 1, 1)
                        if u == 16:
                            hidden_hi(e, 1)
                        if u == 17 and not last:
                            rows_hi(e + 1, 2)
                            rows_hi(e + 1, 3)
                        if u in (18, 21):
                            c = 0 if u == 18 else 2
                            if c == 0:
                                if p:
                                    act.wait_ge(fin_done, TT)
                                act.wait_ge(held_done, e * 4 + (p * (4 * NE - 1) + 1))
                            act.wait_ge(unit_used, e * NEU + (base + u + 1))
                            a(ysb[:, 512 * c:512 * c + 512], mis[:, 0], ACT.Copy).then_inc(ya_out, 1)

                for u in range(SPL):
                    hi2(0, u)
                for b in range(4):
                    rows_hi(0, b)
                with act.Fori(0, NE - 1) as e:
                    body(e, False)
                body(NE - 1, True)

            experts(0)
            overflow(act, lambda: experts(1))

        @block.vector
        def _(dve):
            v = nc.vector
            link = chain(dve, dve_chain)
            own = link.own
            tt_, ts, stt = v.tensor_tensor, v.tensor_scalar, v.scalar_tensor_tensor

            def rsqrt_mean(x, n):
                w = x.shape[1]
                y, t = sm[:, 64:64 + w], sm[:, 80:80 + w]
                link(ts(x, x, 1.0 / n, EPS, ALU.mult, ALU.add))
                link(ts(y.bitcast(I32), x.bitcast(I32), -0.5, float(0x5F3759DF), ALU.mult, ALU.add))
                for step in range(3):
                    link(tt_(t, y, y, ALU.mult))
                    link(stt(t, t, -0.5, x, ALU.mult, ALU.mult))
                    link(stt(y if step < 2 else x, t, 1.5, y, ALU.add, ALU.mult))

            for tt in range(TT):
                dve.wait_ge(rms_sum, tt + 1)
                rsqrt_mean(rstd[:, tt:tt + 1], D)
                if tt == 0:
                    dve.wait_ge(n1_in, 16)
                stt(x0[:, tt], x0[:, tt], rstd[:, tt:tt + 1], n1b[:], ALU.mult, ALU.mult).then_inc(x_scaled, 1)
                own(x_scaled)
            for tt in range(TT):
                dve.wait_ge(x_hi, tt + 1)
                tt_(view(xl, tt * P, [[S, KT], [1, P]]), view(mis if tt == 0 else acc, 0, [[P, KT], [1, P]]),
                    view(xh, tt * P, [[S, KT], [1, P]]).bitcast(F32), ALU.subtract).then_inc(x_ready, 1)
                own(x_ready)

            def lo(n):
                dve.wait_ge(hi_ready, n + 1)
                tt_(wlo[:, n % SPL], raw[:, n % RAW], whi[:, n % SPL].bitcast(F32), ALU.subtract
                    ).then_inc(lo_ready, 1)
                own(lo_ready)

            def s5_prep(part):
                re, im, dt, mag, arg, sin, half, t0, t1, fr, fi, dn = (st[:, k] for k in range(12))
                if part == 0:
                    dve.wait_ge(s_load, 16 * N_SLOAD)
                    link(tt_(lamv[:, 0], lamv[:, 0], lamv[:, 1], ALU.mult))
                    link(tt_(lamv[:, 2], lamv[:, 2], lamv[:, 3], ALU.mult))
                    link(v.tensor_reduce(sm[:, 32:34], view(lamv, 0, [[2 * DK, 2], [1, DK]]), AX_X, ALU.add))
                    v.tensor_copy(sm[:, 36:37], sm[:, 32:33]).then_inc(lam_sum, 1)
                    own(lam_sum)
                    link(ts(qg, qg, DK ** -0.5, None, ALU.mult))
                    link(ts(hg, hg, 1.0 - LAM_INIT, None, ALU.mult))
                    link(ts(c_in[:, 1], c_in[:, 1], -1.0, None, ALU.mult))
                    for d in range(2):
                        link(v.memset(cbd[d][:], 0.0))
                        link(v.memset(H[d][:, 0], 0.0))
                if part == 1:
                    dve.wait_ge(s5_dt, 1)
                    link(tt_(arg, im, dt, ALU.mult))
                    link(ts(t0, arg, 1.0 / (2 * math.pi), 12582912.0, ALU.mult, ALU.add))
                    link(ts(t0, t0, -12582912.0, None, ALU.add))
                    for turn in (-6.28125, -0.0019350051879882812, -3.0199159819567e-07):
                        link(stt(arg, t0, turn, arg, ALU.mult, ALU.add))
                    link(ts(arg, arg, math.pi * (1 - 2 ** -23), -math.pi * (1 - 2 ** -23), ALU.min, ALU.max))
                    tt_(mag, re, dt, ALU.mult).then_inc(s5_arg, 1)
                    own(s5_arg)
                if part == 3:
                    dve.wait_ge(lam_exp, 1)
                    link(tt_(lam, sm[:, 34:35], sm[:, 35:36], ALU.subtract))
                    link(ts(lam, lam, -1.0, -LAM_INIT, ALU.mult, ALU.add))
                    dve.wait_ge(s5_sin, 3)
                    link(v.memset(view(pw, 0, [[1, GRP]]), 1.0))
                    link(v.memset(view(pw, GRP, [[1, GRP]]), 0.0))
                    a1r, a1i = pw[:, 1, 0], pw[:, 1, 1]
                    link(tt_(t0, half, half, ALU.mult))
                    link(ts(t0, t0, -2.0, 1.0, ALU.mult, ALU.add))
                    link(tt_(a1r, mag, t0, ALU.mult))
                    link(tt_(a1i, mag, sin, ALU.mult))
                    link(ts(t0, a1r, -1.0, None, ALU.add))
                    link(tt_(dn, re, re, ALU.mult))
                    link(tt_(t1, im, im, ALU.mult))
                    link(tt_(dn, dn, t1, ALU.add))
                    link(v.reciprocal(dn, dn))
                    link(tt_(fr, t0, re, ALU.mult))
                    link(tt_(t1, a1i, im, ALU.mult))
                    link(tt_(fr, fr, t1, ALU.add))
                    link(tt_(fr, fr, dn, ALU.mult))
                    link(tt_(fi, a1i, re, ALU.mult))
                    link(tt_(t1, t0, im, ALU.mult))
                    link(tt_(fi, fi, t1, ALU.subtract))
                    link(tt_(fi, fi, dn, ALU.mult))
                if part == 4:
                    for have in (1, 2, 4):
                        def src(ri, k0, cnt, step=2 * GRP):
                            return view(pw, (2 * k0 + ri) * GRP, [[step, cnt], [1, GRP]])
                        a_re, a_im = src(0, have, have, 0), src(1, have, have, 0)
                        b_re, b_im = src(0, 1, have), src(1, 1, have)
                        o_re, o_im = src(0, have + 1, have), src(1, have + 1, have)
                        q0 = view(vtmp, 0, [[GRP, have], [1, GRP]])
                        link(cmul(v, link, o_re, o_im, a_re, a_im, b_re, b_im, q0))
                    for d in range(2):
                        link(ts(view(a8, d * 64, [[1, 32]]), view(pw, 17 * GRP + 32 * d, [[1, 32]]), -1.0, None, ALU.mult))
                        link(v.tensor_copy(view(a8, d * 64 + 32, [[1, 32]]), view(pw, 17 * GRP + 32 * d, [[1, 32]])))
                    v.tensor_copy(sm[:, 36:37], sm[:, 32:33]).then_inc(pw_ready, 1)
                    own(pw_ready)

            def norm_heads(x, n_heads, width, sq, stat):
                xv = x.rearrange("p (h e) -> p h e", h=n_heads)
                link(tt_(sq, x, x, ALU.mult))
                link(v.tensor_reduce(stat, sq.rearrange("p (h e) -> p h e", h=n_heads), AX_X, ALU.add))
                rsqrt_mean(stat, width)
                return tt_(xv, xv, stat.unsqueeze(2).broadcast_to([P, n_heads, width]), ALU.mult)

            for n in range(NU + 4):
                if n < NU:
                    lo(n)
                if PREP <= n < PREP + 5:
                    s5_prep(n - PREP)
                if n == A0 + NA + LAG + 2:
                    dve.wait_ge(lag0_in, 16)
                    tt_(ks[0][96:128], ks[0][96:128], lag0[96:128], ALU.add).then_inc(lag0_sum, 1)
                    own(lag0_sum)
                    dve.wait_ge(lag0_sum, 1)
                    v.memset(hb[:], 0.0).then_inc(lag0_sum, 1)
                    own(lag0_sum)
                for b in range(len(BLOCKS)):
                    if n != LAST[b] + LAG:
                        continue
                    if B_Q <= b < B_V:
                        dve.wait_ge(unit_used, LAST[b] + 1)
                        v.tensor_copy(qk[:, :, 512 * (b - B_Q):512 * (b - B_Q) + 512],
                                      view(acc, 1024 * (b % 2), [[512, 2], [1, 512]])).then_inc(acc_free[b % 2], 1)
                        own(acc_free[b % 2], b // 2 + 1)
                    elif B_AT <= b < B_SS:
                        f = b - B_AT
                        dve.wait_ge(unit_used, LAST[b] + 1)
                        g = gA[:, 4 * f:4 * f + 4].rearrange("p f t -> p (f t)")
                        tt_(g, g, acc_of(b), ALU.mult).then_inc(acc_free[b % 2], 1)
                        own(acc_free[b % 2], b // 2 + 1)
                    elif B_SS <= b < B_OUT:
                        f = b - B_SS
                        dve.wait_ge(unit_used, LAST[b] + 1)
                        g = gB[:, 4 * f:4 * f + 4].rearrange("p f t -> p (f t)")
                        ga = gA[:, 4 * f:4 * f + 4].rearrange("p f t -> p (f t)")
                        tt_(g, g, acc_of(b), ALU.mult).then_inc(acc_free[b % 2], 1)
                        own(acc_free[b % 2], b // 2 + 1)
                        evacuated(dve, b)
                        tt_(g, g, ga, ALU.add).then_inc(merged, 1)
                        own(merged)
                    elif b >= B_OUT:
                        f = b - B_OUT
                        dve.wait_ge(unit_used, LAST[b] + 1)
                        if f == 0:
                            dve.wait_ge(x_back, 32)
                        xv = xn[:, :, 512 * f:512 * f + 512]
                        tt_(xv, view(acc, 1024 * (b % 2), [[512, 2], [1, 512]]), xv, ALU.add
                            ).then_inc(acc_free[b % 2], 1)
                        own(acc_free[b % 2], b // 2 + 1)
                if n == LAST[B_OUT] + LAG:
                    dve.wait_ge(r_load, 96)
                    tt_(wr[:], wr[:], view(n2f, 0, [[1, KT], [0, NL]]), ALU.mult).then_inc(wr_scaled, 1)
                    own(wr_scaled)
                i = n - A0 - 1 - LAG
                if 0 <= i < NA:
                    d, ch = i % 2, i // 2
                    dve.wait_ge(in_done, i + 1)
                    for g2 in range(2):
                        o = (view(H[d], 64 + PC * ch, [[1, PC], [PAIRS, 2], [64, CHUNKS]], 64 * g2, 64) if d == 0 else
                             view(H[d], 64 * 32 + PC * ch, [[1, PC], [PAIRS, 2], [-64, CHUNKS]], 64 * g2, 64))
                        ins = v.tensor_copy(o, view(mis, 1024 + 32 * g2, [[128, PC], [64, 2], [1, CHUNKS]],
                                                    64 * g2, 64))
                    ins.then_inc(s_out, 1)
                    own(s_out)
                i = n - A0 - LAG + 2
                if 0 <= i < NA and i % 2 == 0:
                    if i == 0:
                        dve.wait_ge(bb_ready, 1)
                    else:
                        dve.wait_ge(lag_done, i - 1)
                    v_build(v, link, i, vtmp)
                i = n - (A0 + NA + LAG + 1)
                if 0 <= i < 6:
                    if i == 0:
                        dve.wait_ge(s_out, NA)
                    scan_steps(v, link, 0, stepf, CHUNKS * i // 6, CHUNKS * (i + 1) // 6)
                for half, b in enumerate((B_Q, B_K)):
                    for tt in range(TT):
                        if n == LAST[b + 1] + LAG + 1 + tt:
                            evacuated(dve, b)
                            evacuated(dve, b + 1)
                            norm_heads(qk[:, tt, half * AW:(half + 1) * AW], 2 * HEADS, DK,
                                       vtmp[:].rearrange("p a b -> p (a b)"), hs_
                                       ).then_inc([q_norm, k_norm][half], 1)
                            own([q_norm, k_norm][half])
                ch = n - B0 - LAG
                if 0 <= ch < NPC:
                    dve.wait_ge(out_done, ch + 1)
                    uv = U[:, 2 * PC * ch:2 * PC * (ch + 1)]
                    link(tt_(uv, uv, view(dsk, 2 * PC * ch, [[1, 2 * PC], [0, CHUNKS]]), ALU.mult))
                    tt_(uv, uv, view(mis, 512 * (ch % 2), [[CHUNKS, 2 * PC], [1, CHUNKS]]), ALU.add
                        ).then_inc(y_out, 1)
                    own(y_out)
                ch = n - B0 - LAG + 1
                if 0 <= ch < NPC:
                    if ch == 0:
                        dve.wait_ge(k_stored, 16 * 15)
                    else:
                        dve.wait_ge(out_done, ch)
                    z_build(v, link, 0, ch, ztmp[0])
                h = n - H0 - LAG - 1
                if 0 <= h < HEADS:
                    dve.wait_ge(p_ready, 4 * (h + 1))
                    link(v.reciprocal(den, den))
                    link(ts(den[:, 2:4], den[:, 2:4], lam, None, ALU.mult))
                    if h:
                        dve.wait_ge(w_turned, h)
                    for qt in range(TT):
                        link(ts(wm[:, qt], sc[:, 0, qt], den[:, qt:qt + 1], None, ALU.mult))
                        ins = stt(wm[:, qt], sc[:, 1, qt], den[:, 2 + qt:3 + qt], wm[:, qt], ALU.mult, ALU.add)
                        if qt == 0:
                            link(ins)
                    ins.then_inc(w_ready, 1)
                    own(w_ready)
                h = n - H0 - LAG
                if 0 <= h < HEADS:
                    dve.wait_ge(sc_done, h + 1)
                    if h == 0:
                        dve.wait_ge(out_done, NPC)
                    else:
                        dve.wait_ge(w_ready, h)
                    for m in range(2):
                        link(stt(sc[:, m].rearrange("p a b -> p (a b)"), dist[:], -(2.0 ** -(h + 1)),
                                 view(mis, 512 * m, [[1, 512]]), ALU.mult, ALU.add))
                    v.tensor_reduce(nmx, sc[:].rearrange("p m q k -> p (m q) k"), AX_X, ALU.max, negate=True
                                    ).then_inc(sc_out, 1)
                    own(sc_out)
                if n == H0 + 13:
                    dve.wait_ge(g_hi, 1)
                    tt_(gl[:], yT[:], gh[:].bitcast(F32), ALU.subtract).then_inc(g_ready, 1)
                    own(g_ready)
                if n == OT - 1:
                    dve.wait_ge(o_out, HEADS)
                    norm_heads(orow[:].rearrange("p t h e -> p (t h e)"), TT * HEADS, DV,
                               osq[:].rearrange("p t h e -> p (t h e)"), hs_).then_inc(o_norm, 1)
                    own(o_norm)
                if n == OT + LAG:
                    dve.wait_ge(o_hi, 1)
                    stt(ol[:].rearrange("p h t -> p (h t)"), view(mis, 0, [[1, 2048]]), hg,
                        oh[:].bitcast(F32).rearrange("p h t -> p (h t)"), ALU.mult, ALU.subtract).then_inc(o_ready, 1)
                    own(o_ready)
                for f in range(2):
                    if n == LAST[B_GLU + f] + LAG:
                        evacuated(dve, B_GLU + f)
                        y = yT[:, 4 * f:4 * f + 4]
                        tt_(y, y, sg[:, 4 * f:4 * f + 4], ALU.mult).then_inc(glu_s, 1)
                        own(glu_s)
                    if n == LAST[B_GLU + f] + LAG + 1:
                        dve.wait_ge(s_hi, f + 1)
                        tt_(sl[:, 4 * f:4 * f + 4], yT[:, 4 * f:4 * f + 4], sh[:, 4 * f:4 * f + 4].bitcast(F32),
                            ALU.subtract).then_inc(s_ready, 1)
                        own(s_ready)
                for f in range(4):
                    if n == LAST[B_SS + f] + LAG + 1:
                        dve.wait_ge(m_hi, f + 1)
                        tt_(ml[:, 4 * f:4 * f + 4], gB[:, 4 * f:4 * f + 4], mh[:, 4 * f:4 * f + 4].bitcast(F32),
                            ALU.subtract).then_inc(m_ready, 1)
                        own(m_ready)

            dve.wait_ge(ssq_out, 2 * 4)
            link(v.tensor_reduce(rstd, view(ssq, 0, [[4, TT], [1, 4]]), AX_X, ALU.add))
            rsqrt_mean(rstd, D)
            v.tensor_copy(ssq[:, 0:TT], rstd).then_inc(rstd_ready, 1)

            def r2(off, n=NG, inner=None):
                return view(rt, off, [[n, TT], [1, n]])

            def rb_(off, n=NG):
                return view(rt, off, [[1, TT], [0, n]])
            LG, T, TB, OH, O1, O2, VA, VB, M1, M2, RK = 96, 64, 136, 144, 152, 160, 168, 170, 176, 208, 240
            GW, DD, ES, EX, ROW, RANK, BASE, KEEP, HELD = 172, 80, 272, 84, 336, 400, 404, 408, 416
            dve.wait_ge(logits, 1)
            for tt in range(TT):
                link(stt(view(rt, LG + NL * tt, [[1, NL]]), view(mis, 1024 + 32 * tt, [[1, NL]]), rstd[:, tt:tt + 1],
                         rb[:], ALU.mult, ALU.add))
            gl_ = view(rt, LG, [[NL, TT], [1, NG]])
            order = view(rcs, TT, [[0, TT], [1, NG]])

            def first_max(x, top, hot):
                link(v.tensor_reduce(view(rt, top, [[1, TT]]), x, AX_X, ALU.max))
                link(tt_(r2(hot), x, rb_(top), ALU.is_equal))
                link(tt_(r2(hot), r2(hot), order, ALU.mult))
                link(v.tensor_reduce(view(rt, TB, [[1, TT]]), r2(hot), AX_X, ALU.max))
                link(tt_(r2(hot), r2(hot), rb_(TB), ALU.is_equal))

            first_max(gl_, VA, OH)
            tt_(r2(T), gl_, rb_(VA), ALU.subtract).then_inc(r_arg, 1)
            own(r_arg)
            link(tt_(view(rt, ES, [[16, TT], [4, EG], [1, NG]]), view(rt, LG + NG, [[NL, TT], [1, EG], [EG, NG]]),
                     view(rt, OH, [[NG, TT], [0, EG], [1, NG]]), ALU.mult))
            link(v.tensor_reduce(view(rt, ROW, [[4, TT], [1, EG]]), view(rt, ES, [[16, TT], [4, EG], [1, NG]]),
                                 AX_X, ALU.add))
            first_max(r2(ROW), VA, O1)
            link(stt(r2(ROW + 8), r2(O1), -3.0e38, r2(ROW), ALU.mult, ALU.add))
            first_max(r2(ROW + 8), VB, O2)
            tt_(view(rt, DD, [[1, TT]]), view(rt, VB, [[1, TT]]), view(rt, VA, [[1, TT]]), ALU.subtract
                ).then_inc(r_arg, 1)
            own(r_arg)
            for m, o in ((M1, O1), (M2, O2)):
                link(tt_(view(rt, m, [[NE, TT], [EG, NG], [1, EG]]), view(rt, OH, [[NG, TT], [1, NG], [0, EG]]),
                         view(rt, o, [[EG, TT], [0, NG], [1, EG]]), ALU.mult))
            tt_(view(rt, 0, [[1, TT * NE]]), view(rt, M1, [[1, TT * NE]]), view(rt, M2, [[1, TT * NE]]), ALU.add
                ).then_inc(mask_ready, 1)
            own(mask_ready)
            dve.wait_ge(rank_done, 1)
            flat = [[1, TT * NE]]
            link(v.tensor_copy(view(rt, RK, flat), view(mis, 512, flat)))
            link(stt(view(rt, HELD, flat), view(rt, RK, flat), 1.0, view(rt, 0, flat), ALU.add, ALU.mult))
            link(ts(view(rt, HELD, flat), view(rt, HELD, flat), -1.0, None, ALU.add))

            def fill_slots(p):
                if p:
                    dve.wait_ge(rc2_in, 16)
                slots = view(rc2, 0, [[0, NE], [1, P]]) if p else view(rc, 2 * P, [[0, NE], [1, P]])
                for tt in range(TT):
                    ins = tt_(sel[:, tt], slots, view(rt, HELD + NE * tt, [[1, NE], [0, P]]), ALU.is_equal)
                ins.then_inc(sel_ready, 1)

            fill_slots(0)
            dve.wait_ge(r_exp, 2)
            one = view(rt, EX, [[1, TT]])
            link(v.tensor_reduce(one, r2(T), AX_X, ALU.add))
            link(v.reciprocal(one, one))
            ex, t2 = view(rt, DD, [[1, TT]]), view(rt, TB, [[1, TT]])
            link(ts(t2, ex, 1.0, None, ALU.add))
            link(v.reciprocal(t2, t2))
            link(tt_(wts[:, 0:TT], t2, one, ALU.mult))
            link(tt_(wts[:, TT:2 * TT], wts[:, 0:TT], ex, ALU.mult))
            link(v.tensor_reduce(view(rt, TB, [[1, 1]]), view(mis, 512 + 2 * NE, [[1, NE]]), AX_X, ALU.max))
            link(ts(flag[:, 0:1], view(rt, TB, [[1, 1]]), SLOTS + 0.5, None, ALU.is_gt))
            link(ts(flag[:, 1:2], view(rt, TB, [[1, 1]]), HALF + 0.5, None, ALU.is_gt))
            link(ts(view(rt, KEEP, [[1, 1]]), view(rt, TB, [[1, 1]]), HALF + 0.5, None, ALU.is_gt))
            link(ts(view(rt, KEEP, [[1, 1]]), view(rt, KEEP, [[1, 1]]), 0.5, 0.5, ALU.mult, ALU.add))
            for c, m in enumerate((M1, M2)):
                for out, x in ((RANK, view(rt, RK, [[NE, TT], [1, NE]])),
                               (BASE, view(rcs, TT + NG, [[0, TT], [1, NE]]))):
                    link(tt_(view(rt, ES, [[NE, TT], [1, NE]]), x, view(rt, m, [[NE, TT], [1, NE]]), ALU.mult))
                    link(v.tensor_reduce(view(rt, out + TT * c, [[1, TT]]), view(rt, ES, [[NE, TT], [1, NE]]),
                                         AX_X, ALU.add))
            link(ts(view(rt, BASE, [[1, 2 * TT]]), view(rt, BASE, [[1, 2 * TT]]), rt[:, KEEP:KEEP + 1], None, ALU.mult))
            v.tensor_copy(wts[:, 0:1], wts[:, 0:1]).then_inc(routed, 1)
            own(routed)

            dve.nop().then_inc(yd_out, 1)

            def experts(p):
                base, q = NU + p * NE * NEU, p * NE
                four = [[1, 2 * TT]]
                keep = view(rt, KEEP, four)
                link(ts(keep, view(rt, RANK, four), SLOTS - 0.5, None, ALU.is_gt if p else ALU.is_lt))
                link(tt_(wtp[:], wts[:], keep, ALU.mult))
                if p:
                    link(ts(view(rt, RANK, four), view(rt, RANK, four), -float(SLOTS), None, ALU.add))
                link(tt_(keep, keep, view(rt, RANK, four), ALU.mult))
                link(tt_(keep, keep, view(rt, BASE, four), ALU.add))
                v.tensor_copy(rows[:], keep).then_inc(rows_ready, 1)
                own(rows_ready)
                for i, (e0, e1) in enumerate(((0, 1), (1, NE))):
                    dve.wait_ge(idx_done, 2 * p + i + 1)
                    v.tensor_copy(idx[:, e0:e1], view(mis, (0 if i else 1024) + e0, [[1, e1 - e0]])).then_inc(idx_ready, 1)

                def lo2(e, u):
                    dve.wait_ge(hi_ready, e * NEU + (base + u + 1))
                    tt_(wlo[:, (base + u) % SPL], slot(u % RAW2), whi[:, (base + u) % SPL].bitcast(F32), ALU.subtract
                        ).then_inc(lo_ready, 1)

                def rows_lo(e, b):
                    dve.wait_ge(gT_hi, e * 4 + (4 * q + b + 1))
                    tt_(gTl[:, 4 * b:4 * b + 4], mis[:, GB_OF[b]].rearrange("p (k t) -> p k t", t=P),
                        gTh[:, 4 * b:4 * b + 4].bitcast(F32), ALU.subtract).then_inc(gT_ready, 1)

                def hidden_lo(e, f):
                    dve.wait_ge(hT_hi, e * 2 + (2 * q + f + 1))
                    tt_(hTl[:, 4 * f:4 * f + 4], mis[:, 2 + f].rearrange("p (k t) -> p k t", t=P),
                        hTh[:, 4 * f:4 * f + 4].bitcast(F32), ALU.subtract).then_inc(hT_ready, 1)

                def body(e, last):
                    for u in range(NEU):
                        if u + SPL < NEU:
                            lo2(e, u + SPL)
                        elif not last:
                            lo2(e + 1, u + SPL - NEU)
                        if u in (7, 15):
                            f = u // 8
                            dve.wait_ge(silu_done, e * 2 + (2 * q + f + 1))
                            tt_(hid[:, f], sgm[:, f], acc[:, 2 * f + 1], ALU.mult).then_inc(hid_ready, 1)
                        if u == 11:
                            hidden_lo(e, 0)
                        if u == 15 and not last:
                            rows_lo(e + 1, 0)
                            rows_lo(e + 1, 1)
                        if u == 16:
                            hidden_lo(e, 1)
                        if u == 17 and not last:
                            rows_lo(e + 1, 2)
                            rows_lo(e + 1, 3)
                        if u in (19, 23):
                            c = 1 if u == 19 else 3
                            if c == 1:
                                dve.wait_ge(held_done, e * 4 + (p * (4 * NE - 1) + 1))
                            dve.wait_ge(unit_used, e * NEU + (base + u + 1))
                            v.tensor_copy(ysb[:, 512 * c:512 * c + 512], mis[:, 1]).then_inc(yd_out, 1)

                if p == 0:
                    dve.wait_ge(first_split, 1)
                else:
                    for u in range(SPL):
                        lo2(0, u)
                for b in range(4):
                    rows_lo(0, b)
                with dve.Fori(0, NE - 1) as e:
                    body(e, False)
                body(NE - 1, True)
                for tt in range(TT):
                    dve.wait_ge(fin_in[tt], 32 * (p + 1))
                    link(stt(xn[:, tt], fin[tt][:, 0], wtp[:, tt:tt + 1], xn[:, tt], ALU.mult, ALU.add))
                    stt(xn[:, tt], fin[tt][:, 1], wtp[:, TT + tt:TT + tt + 1], xn[:, tt], ALU.mult, ALU.add
                        ).then_inc(fin_done, 1)
                    own(fin_done)

            experts(0)
            def again():
                fill_slots(1)
                experts(1)
            overflow(dve, again)
        @block.gpsimd
        def _(pool):
            g = nc.gpsimd
            link = chain(pool, pool_chain)
            own = link.own
            link(g.memset(lag0[96:128], 0.0))
            pool.wait_ge(s_load, 16 * N_SLOAD)
            pool.wait_ge(pw_ready, 1)
            for d in range(2):
                fr, fi = (view(st, k * GRP + 32 * d, [[1, 32], [0, GP]]) for k in (9, 10))
                br, bi = (view(b_in, (ri * GRP + 32 * d) * GP, [[GP, 32], [1, GP]]) for ri in range(2))
                orr, oi = (view(bb, (ri * GRP + 32 * d) * GP, [[GP, 32], [1, GP]]) for ri in range(2))
                ins = cmul(g, link, orr, oi, fr, fi, br, bi, view(ptmp, 0, [[GP, 32], [1, GP]]))
                if d == 0:
                    link(ins)
            ins.then_inc(bb_ready, 1)
            own(bb_ready)
            pool.wait_ge(bb_ready, 1)
            for ch in range(NPC):
                i = 2 * ch + 1
                if ch:
                    pool.wait_ge(lag_done, i - 1)
                v_build(g, link, i, ptmp)
            pool.wait_ge(s_out, NA)
            scan_steps(g, link, 1, ptmp, 0, CHUNKS)
            pool.wait_ge(scan_done[1], 1)
            pool.wait_ge(k_stored, 16 * 15)
            for ch in range(NPC):
                if ch:
                    pool.wait_ge(out_done, ch)
                z_build(g, link, 1, ch, ztmp[1])
            pool.wait_ge(r_load, 96)
            for tt in range(TT):
                pool.wait_ge(x2_scaled, tt + 1)
                g.tensor_tensor(x2[tt][:], x2[tt][:], n2b[:], ALU.mult).then_inc(x2_ready, 1)
                pool.wait_ge(x2_ready, tt + 1)
                pool.dma_start(xd[tt * P:(tt + 1) * P], x2[tt][:]).then_inc(x2_stored, 16)
            def split_first(u):
                pool.wait_ge(hi_ready, NU + u + 1)
                g.tensor_tensor(wlo[:, (NU + u) % SPL], slot(u), whi[:, (NU + u) % SPL].bitcast(F32), ALU.subtract
                                ).then_inc(lo_ready, 1)

            split_first(0)
            pool.wait_ge(x2_stored, 32)
            pool.wait_ge(routed, 1)
            g.memset(xg[:], 0.0).then_inc(xg_clear, 1)
            pool.wait_ge(xg_clear, 1)
            many = pool.value_load(flag[0:1, 1:2], min_val=0, max_val=1)

            def sized(p, body):
                if p:
                    return body(SLOTS)
                for slots, taken in ((SLOTS, many > 0), (HALF, many < 1)):
                    with pool.If(taken):
                        body(slots)
                        pool.nop()

            def experts(p):
                q = p * NE
                pool.wait_ge(idx_ready, 2 * p + 1)

                def hold(count):
                    if not (p == 0 and isinstance(count, int) and count == 0):
                        pool.wait_ge(held_done, count + p * (4 * NE - 1))
                    g.tensor_tensor(held[:], ident[:, 0:1], ident[:, 0:1], ALU.mult).then_inc(held_done, 1)

                def gather(e, col, first=False):
                    if not first:
                        pool.wait_ge(xg_turned, e * 4 + 4 * q)
                        hold(e * 4 - 3)
                    g.tensor_copy(idxc[:], col).then_inc(idxc_ready, 1)
                    pool.wait_ge(idxc_ready, e + (q + 1))
                    hold(0 if first else e * 4 - 2)

                    def rows_in(n):
                        g.indirect_dma_start(xg[0:n], None, xd, bass.IndirectOffsetOnAxis(ap=idxc[0:n, 0:1], axis=0)
                                             ).then_inc(xg_in, 16)
                    sized(p, rows_in)

                def body(e, last):
                    if not last:
                        gather(e + 1, idx[:, bass.ds(e + 1, 1)])
                    pool.wait_ge(ya_out, e * 2 + (2 * q + 3))
                    pool.wait_ge(yd_out, e * 2 + (2 * q + 3))
                    hold(e * 4 + (1 if last else 3))

                    def rows_out(n):
                        pool.dma_start((yr if n == SLOTS else yh)[bass.ds(e * n, n)], ysb[0:n]).then_inc(y_kept, 16)
                    sized(p, rows_out)
                    pool.wait_ge(y_kept, e * 16 + (16 * q + 16))
                    hold(e * 4 + (2 if last else 4))

                gather(0, idx[:, 0:1], first=True)
                if p == 0:
                    for u in range(1, SPL):
                        split_first(u)
                    pool.wait_ge(lo_ready, NU + SPL)
                    pool.nop().then_inc(first_split, 1)
                pool.wait_ge(idx_ready, 2 * p + 2)
                with pool.Fori(0, NE - 1) as e:
                    body(e, False)
                body(NE - 1, True)
                
                pool.wait_ge(rows_ready, p + 1)

                def rows_back(n):
                    for tt in range(TT):
                        for c in range(2):
                            g.indirect_dma_start(fin[tt][:, c], None, yr if n == SLOTS else yh,
                                                 bass.IndirectOffsetOnAxis(ap=rows[:, TT * c + tt:TT * c + tt + 1],
                                                                           axis=0)).then_inc(fin_in[tt], 16)
                sized(p, rows_back)

            experts(0)
            overflow(pool, lambda: experts(1))
_WEIGHTS = ("w_in", "w_glu", "w_attn_up", "w_ssm_up", "w_out")


def _constants(np):
    j = np.arange(S)
    t = STEPS * (j % CHUNKS) + j // CHUNKS
    dist = np.abs(t[:, None] - t[None, :]).astype(np.float32)
    return {
        "ident": np.eye(P, dtype=np.float32),
        "router_tables": np.concatenate([np.triu(np.ones((P, P)), 1), np.ones((P, P)),
                                         np.tile(np.arange(S), (P, 1))], 1).astype(np.float32),
        "router_rows": np.concatenate([np.arange(S).reshape(TT, P).T, np.tile(np.arange(NG, 0, -1), (P, 1)),
                                       np.tile(SLOTS * np.arange(NE), (P, 1))], 1).astype(np.float32),
        "dist": dist.reshape(TT, P, S).transpose(1, 0, 2).reshape(P, TT * S),
    }


def _lay_out(np, inputs):
    g = {k: np.asarray(v) for k, v in inputs.items()}
    out = {"x": g["x"].reshape(CHUNKS, STEPS, D).transpose(1, 0, 2).reshape(S, D)}
    for w in _WEIGHTS:
        out[w] = g[w][0]
    for w in ("w1", "w3", "w2"):
        out[w] = g[w][0]
    out["norm2"] = g["norm2"].reshape(1, D)
    out["norm2_features"] = g["norm2"].reshape(KT, P).T
    r = np.concatenate([g["w_router_group"][0], g["w_router_expert"][0]], 1)
    out["w_router"] = r.reshape(KT, P, NG + NE).transpose(1, 0, 2)
    out["b_router"] = np.concatenate([g["b_router_group"], g["b_router_expert"]], 1)
    out["norm1"] = g["norm1"].reshape(1, D)
    for k in ("q_gain", "k_gain"):
        out[k] = g[k].reshape(DK, 1)
    out["head_gain"] = g["head_gain"].reshape(DV, 1)
    for k in ("lam_q1", "lam_k1", "lam_q2", "lam_k2"):
        out[k] = g[k].reshape(1, DK)
    for k, n in (("ssm_lam_re", "lam_re"), ("ssm_lam_im", "lam_im")):
        out[n] = g[k].reshape(2, PAIRS, 2, NST).transpose(2, 3, 0, 1).reshape(P, GRP)
    out["log_dt"] = g["ssm_log_dt"].reshape(2, PAIRS, 2).transpose(2, 0, 1).reshape(2, GRP)
    b = np.stack([g["ssm_b_re"], g["ssm_b_im"]]).reshape(2, 2, PAIRS, 2, NST, GP)
    out["b"] = b.transpose(0, 3, 4, 1, 2, 5).reshape(2, P, GRP * GP)
    c = np.stack([g["ssm_c_re"], g["ssm_c_im"]]).reshape(2, 2, PAIRS, 2, GP, NST)
    out["c"] = c.transpose(0, 3, 5, 1, 2, 4).reshape(2, P, GRP * GP)
    out["d_skip"] = g["ssm_d"].reshape(GRP, GP).T
    return out


def kernel(**inputs):
    import numpy as _np
    import concourse.bacc as _bacc
    from concourse.bass_utils import run_bass_kernel_spmd as _run

    nc = _bacc.Bacc("TRN2", target_bir_lowering=False, num_devices=1)
    arrays, io = {}, {}
    laid = {**_constants(_np), **_lay_out(_np, inputs)}
    for name, a in laid.items():
        a = _np.ascontiguousarray(a)
        arrays["in_" + name] = a
        io[name] = nc.dram_tensor("in_" + name, a.shape, mybir.dt.from_np(a.dtype), kind="ExternalInput").ap()
    io["out"] = nc.dram_tensor("out_dram", (S, D), F32, kind="ExternalOutput").ap()
    encoder(nc, io)
    r = _run(nc, [arrays], core_ids=[0])
    y = r.results[0]["out_dram"]
    return y.reshape(STEPS, CHUNKS, D).transpose(1, 0, 2).reshape(1, S, D)
```
